# Optimizing a Trainium2 kernel written in Bass

```python
import math
import jax, jax.numpy as jnp
from jax import lax
import numpy as np
import jax
import jax.numpy as jnp

D_MODEL = 1024
BATCH = 1
SEQ = 256
DEPTH = 2

MIX_WIDTH = D_MODEL
GDN_HEADS = 4
GDN_HEAD_DIM = 128
GDN_WIDTH = GDN_HEADS * GDN_HEAD_DIM
GDN_CONV = 4
GDN_CHUNK = 64
NSA_HEADS = 8
NSA_KV_HEADS = 2
NSA_HEAD_DIM = 64
NSA_WIDTH = NSA_HEADS * NSA_HEAD_DIM
NSA_KV_WIDTH = NSA_KV_HEADS * NSA_HEAD_DIM
CMP_LEN = 32
CMP_STRIDE = 16
CMP_HIDDEN = 2 * NSA_HEAD_DIM
SEL_BLOCK = 64
N_SELECT = 16
WINDOW = 512
Q_BLOCK = 128
ROPE_THETA = 500000.0
ROT_DIM = NSA_HEAD_DIM // 4
D_FF = 2816
N_ADA = 9
NORM_EPS = 1e-6
IN_SIZES = (3 * GDN_WIDTH, GDN_WIDTH, GDN_HEADS, GDN_HEADS,
            NSA_WIDTH, NSA_KV_WIDTH, NSA_KV_WIDTH, NSA_KV_WIDTH,
            NSA_KV_WIDTH, NSA_KV_WIDTH, NSA_KV_WIDTH, 3 * NSA_HEADS)
IN_WIDTH = sum(IN_SIZES)


def rms_norm(x, g):
    xf = x.astype(jnp.float32)
    y = xf * lax.rsqrt(jnp.mean(xf * xf, axis=-1, keepdims=True) + NORM_EPS)
    return (y * g.astype(jnp.float32)).astype(x.dtype)

def l2_norm(x):
    xf = x.astype(jnp.float32)
    return xf * lax.rsqrt(jnp.sum(xf * xf, axis=-1, keepdims=True) + NORM_EPS)

def modulate(h, shift, scale):
    return h * (1.0 + scale[:, None, :]) + shift[:, None, :]

def swiglu(h, w_in, w_out):
    gate, up = jnp.split(h @ w_in, 2, axis=-1)
    return (jax.nn.silu(gate) * up) @ w_out

def split_cols(x, sizes):
    offs = [int(o) for o in np.cumsum(sizes)[:-1]]
    return jnp.split(x, offs, axis=-1)

def masked_softmax(s, mask):
    s = jnp.where(mask, s.astype(jnp.float32), -jnp.inf)
    m = jnp.max(s, axis=-1, keepdims=True)
    m = jnp.where(jnp.isfinite(m), m, 0.0)
    p = jnp.exp(s - m)
    return p / jnp.maximum(jnp.sum(p, axis=-1, keepdims=True), 1e-30)

def partial_rope(x, cos, sin):
    half = ROT_DIM // 2
    xf = x[..., :ROT_DIM].astype(jnp.float32)
    x1, x2 = xf[..., :half], xf[..., half:]
    rot = jnp.concatenate([x1 * cos - x2 * sin, x2 * cos + x1 * sin], axis=-1).astype(x.dtype)
    return jnp.concatenate([rot, x[..., ROT_DIM:]], axis=-1)

def causal_dwconv(x, w):
    k = w.shape[0]
    return lax.conv_general_dilated(
        x, w[:, None, :].astype(x.dtype), window_strides=(1,), padding=[(k - 1, 0)],
        dimension_numbers=("NWC", "WIO", "NWC"), feature_group_count=x.shape[-1])

def chunk_gated_delta_rule(q, k, v, g, beta):
    B, T, H, Dk = q.shape
    Dv = v.shape[-1]
    C = GDN_CHUNK
    N = T // C

    def chunks(t):
        t = t.astype(jnp.float32).reshape((B, N, C, H) + t.shape[3:])
        return jnp.moveaxis(t, (1, 3), (0, 2))

    qc, kc, vc, bc = chunks(q), chunks(k), chunks(v), chunks(beta)
    gc = jnp.cumsum(chunks(g), axis=-1)
    causal = jnp.tril(jnp.ones((C, C), dtype=bool))
    strict = jnp.tril(jnp.ones((C, C), dtype=bool), -1)
    decay = jnp.exp(jnp.where(causal, gc[..., :, None] - gc[..., None, :], -jnp.inf))
    kb = kc * bc[..., None]
    lower = jnp.where(strict, jnp.einsum("nbhcd,nbhsd->nbhcs", kb, kc) * decay, 0.0)
    rhs = jnp.concatenate([vc * bc[..., None], kb * jnp.exp(gc)[..., None]], axis=-1)
    sol = lax.linalg.triangular_solve(lower, rhs, left_side=True, lower=True, unit_diagonal=True)
    u, w = sol[..., :Dv], sol[..., Dv:]

    def step(S, xs):
        q_i, k_i, u_i, w_i, g_i, d_i = xs
        v_new = u_i - jnp.einsum("bhcd,bhdv->bhcv", w_i, S)
        attn = jnp.einsum("bhcd,bhsd->bhcs", q_i, k_i) * d_i
        o = (jnp.einsum("bhcd,bhdv->bhcv", q_i * jnp.exp(g_i)[..., None], S)
             + jnp.einsum("bhcs,bhsv->bhcv", attn, v_new))
        g_last = g_i[..., -1:]
        S = (S * jnp.exp(g_last)[..., None]
             + jnp.einsum("bhcd,bhcv->bhdv", k_i * jnp.exp(g_last - g_i)[..., None], v_new))
        return S, o

    S0 = jnp.zeros((B, H, Dk, Dv), jnp.float32)
    _, o = lax.scan(step, S0, (qc, kc, u, w, gc, decay))
    return jnp.moveaxis(o, (0, 2), (1, 3)).reshape(B, T, H, Dv)

def gated_deltanet(qkv, z, b_raw, a_raw, conv_w, a_log, dt_bias, norm_g):
    B, T, _ = qkv.shape
    qkv = jax.nn.silu(causal_dwconv(qkv, conv_w))
    q, k, v = jnp.split(qkv, 3, axis=-1)
    hd = (B, T, GDN_HEADS, GDN_HEAD_DIM)
    q = l2_norm(q.reshape(hd)) * (GDN_HEAD_DIM ** -0.5)
    k = l2_norm(k.reshape(hd))
    v = v.reshape(hd)
    beta = jax.nn.sigmoid(b_raw.astype(jnp.float32))
    g = -jnp.exp(a_log.astype(jnp.float32)) * jax.nn.softplus(a_raw.astype(jnp.float32) + dt_bias.astype(jnp.float32))
    o = chunk_gated_delta_rule(q, k, v, g, beta)
    o = rms_norm(o, norm_g) * jax.nn.silu(z.reshape(hd).astype(jnp.float32))
    return o.reshape(B, T, GDN_WIDTH).astype(qkv.dtype)

def native_sparse_attention(q, kc, vc, ks, vs, kw, vw, gate_raw, cos, sin,
                            pe_k, w1_k, w2_k, pe_v, w1_v, w2_v, out_norm_g):
    B, T, _ = q.shape
    Hq, G, dh = NSA_HEADS, NSA_KV_HEADS, NSA_HEAD_DIM
    R = Hq // G
    scale = dh ** -0.5
    q = partial_rope(q.reshape(B, T, Hq, dh), cos, sin).reshape(B, T, G, R, dh)
    heads = lambda t: t.reshape(B, T, G, dh)
    kc = partial_rope(heads(kc), cos, sin)
    ks = partial_rope(heads(ks), cos, sin)
    kw = partial_rope(heads(kw), cos, sin)
    vc, vs, vw = heads(vc), heads(vs), heads(vw)

    n_cmp = (T - CMP_LEN) // CMP_STRIDE + 1
    cmp_idx = np.arange(n_cmp)[:, None] * CMP_STRIDE + np.arange(CMP_LEN)[None, :]

    def compress(t, pe, w1, w2):
        blk = t[:, cmp_idx] + pe[:, None, :]
        blk = jnp.moveaxis(blk, 3, 2).reshape(B, n_cmp, G, CMP_LEN * dh)
        return jax.nn.silu(blk @ w1) @ w2

    k_cmp = compress(kc, pe_k, w1_k, w2_k)
    v_cmp = compress(vc, pe_v, w1_v, w2_v)
    cmp_end = jnp.asarray(cmp_idx[:, -1])

    n_blk = T // SEL_BLOCK
    n_sel = min(N_SELECT, n_blk)
    sel_start = np.arange(n_blk) * SEL_BLOCK
    overlap = jnp.asarray(((cmp_idx[:, :1] < sel_start[None, :] + SEL_BLOCK)
                           & (cmp_idx[:, -1:] >= sel_start[None, :])).astype(np.float32))
    blk_ids = jnp.arange(n_blk)
    ks_t = jnp.moveaxis(ks, 2, 1)
    vs_t = jnp.moveaxis(vs, 2, 1)
    b_ix = jnp.arange(B)[:, None, None, None]
    g_ix = jnp.arange(G)[None, :, None, None]
    kw_pad = jnp.pad(kw, ((0, 0), (WINDOW, 0), (0, 0), (0, 0)))
    vw_pad = jnp.pad(vw, ((0, 0), (WINDOW, 0), (0, 0), (0, 0)))
    gates = jax.nn.sigmoid(gate_raw.astype(jnp.float32)).reshape(B, T, G, R, 3)

    def one_block(i):
        s = i * Q_BLOCK
        t = s + jnp.arange(Q_BLOCK)
        qb = lax.dynamic_slice_in_dim(q, s, Q_BLOCK, axis=1)
        gb = lax.dynamic_slice_in_dim(gates, s, Q_BLOCK, axis=1)
        sc = jnp.einsum("bqgrd,bngd->bgrqn", qb, k_cmp) * scale
        p_cmp = masked_softmax(sc, cmp_end[None, :] <= t[:, None])
        o_cmp = jnp.einsum("bgrqn,bngd->bqgrd", p_cmp.astype(v_cmp.dtype), v_cmp)
        imp = jnp.einsum("bgrqn,nj->bgqj", p_cmp, overlap)
        cur = t[:, None] // SEL_BLOCK
        forced = (blk_ids == 0) | (blk_ids == cur) | (blk_ids == cur - 1)
        valid = blk_ids * SEL_BLOCK <= t[:, None]
        imp = jnp.where(forced, jnp.inf, jnp.where(valid, imp, -jnp.inf))
        _, top = lax.top_k(imp, n_sel)
        tok = (top[..., None] * SEL_BLOCK + jnp.arange(SEL_BLOCK)).reshape(B, G, Q_BLOCK, n_sel * SEL_BLOCK)
        k_sel = ks_t[b_ix, g_ix, tok]
        v_sel = vs_t[b_ix, g_ix, tok]
        ss = jnp.einsum("bqgrd,bgqld->bgrql", qb, k_sel) * scale
        p_sel = masked_softmax(ss, (tok <= t[:, None])[:, :, None])
        o_sel = jnp.einsum("bgrql,bgqld->bqgrd", p_sel.astype(v_sel.dtype), v_sel)
        k_win = lax.dynamic_slice_in_dim(kw_pad, s, WINDOW + Q_BLOCK, axis=1)
        v_win = lax.dynamic_slice_in_dim(vw_pad, s, WINDOW + Q_BLOCK, axis=1)
        kp = s - WINDOW + jnp.arange(WINDOW + Q_BLOCK)
        win_mask = (kp[None, :] <= t[:, None]) & (kp[None, :] > t[:, None] - WINDOW) & (kp[None, :] >= 0)
        sw = jnp.einsum("bqgrd,bkgd->bgrqk", qb, k_win) * scale
        p_win = masked_softmax(sw, win_mask)
        o_win = jnp.einsum("bgrqk,bkgd->bqgrd", p_win.astype(v_win.dtype), v_win)
        o = gb[..., 0:1] * o_cmp + gb[..., 1:2] * o_sel + gb[..., 2:3] * o_win
        o = rms_norm(o, out_norm_g)
        return o.reshape(B, Q_BLOCK, NSA_WIDTH)

    out = lax.map(one_block, jnp.arange(T // Q_BLOCK))
    return jnp.moveaxis(out, 0, 1).reshape(B, T, NSA_WIDTH).astype(q.dtype)

def token_mix(h, w_in, conv_w, a_log, dt_bias, gdn_norm_g, pe_k, w1_k, w2_k,
              pe_v, w1_v, w2_v, nsa_norm_g, w_out, cos, sin):
    (qkv, z, b_raw, a_raw, q_n, kc, vc, ks, vs, kw, vw, g_raw) = split_cols(h @ w_in, IN_SIZES)
    y_gdn = gated_deltanet(qkv, z, b_raw, a_raw, conv_w, a_log, dt_bias, gdn_norm_g)
    y_nsa = native_sparse_attention(q_n, kc, vc, ks, vs, kw, vw, g_raw, cos, sin,
                                    pe_k, w1_k, w2_k, pe_v, w1_v, w2_v, nsa_norm_g)
    return jnp.concatenate([y_gdn, y_nsa.astype(y_gdn.dtype)], axis=-1) @ w_out

def first_inputs(seed: int = 0) -> dict:
    key = jax.random.key(seed)
    ks = jax.random.split(key, 24)
    nrm = lambda k, shape, s: jax.random.normal(k, shape, jnp.float32) * s
    x = nrm(ks[0], (BATCH, SEQ, D_MODEL), 1.0)
    c = nrm(ks[1], (BATCH, D_MODEL), 1.0)
    positions = (jax.random.randint(ks[2], (BATCH, 1), 0, SEQ, dtype=jnp.int32)
                 + jnp.arange(SEQ, dtype=jnp.int32)[None, :])
    ada_w = nrm(ks[3], (DEPTH, D_MODEL, N_ADA * D_MODEL), 0.5 * D_MODEL ** -0.5)
    ada_b = nrm(ks[4], (DEPTH, N_ADA * D_MODEL), 0.02)
    norm_g = 1.0 + nrm(ks[5], (DEPTH, 3, D_MODEL), 0.02)
    ffn_w_in = nrm(ks[6], (DEPTH, 2, D_MODEL, 2 * D_FF), D_MODEL ** -0.5)
    ffn_w_out = nrm(ks[7], (DEPTH, 2, D_FF, D_MODEL), D_FF ** -0.5)
    mix_w_in = nrm(ks[8], (DEPTH, D_MODEL, IN_WIDTH), D_MODEL ** -0.5)
    gdn_conv_w = nrm(ks[9], (DEPTH, GDN_CONV, 3 * GDN_WIDTH), GDN_CONV ** -0.5)
    gdn_a_log = jnp.log(jax.random.uniform(ks[10], (DEPTH, GDN_HEADS), jnp.float32, 1.0, 16.0))
    dt = jnp.exp(jax.random.uniform(ks[11], (DEPTH, GDN_HEADS), jnp.float32, math.log(1e-3), math.log(1e-1)))
    gdn_dt_bias = dt + jnp.log(-jnp.expm1(-dt))
    gdn_norm_g = 1.0 + nrm(ks[12], (DEPTH, GDN_HEAD_DIM), 0.02)
    cmp_pe_k = nrm(ks[13], (DEPTH, CMP_LEN, NSA_HEAD_DIM), 0.1)
    cmp_w1_k = nrm(ks[14], (DEPTH, CMP_LEN * NSA_HEAD_DIM, CMP_HIDDEN), (CMP_LEN * NSA_HEAD_DIM) ** -0.5)
    cmp_w2_k = nrm(ks[15], (DEPTH, CMP_HIDDEN, NSA_HEAD_DIM), CMP_HIDDEN ** -0.5)
    cmp_pe_v = nrm(ks[16], (DEPTH, CMP_LEN, NSA_HEAD_DIM), 0.1)
    cmp_w1_v = nrm(ks[17], (DEPTH, CMP_LEN * NSA_HEAD_DIM, CMP_HIDDEN), (CMP_LEN * NSA_HEAD_DIM) ** -0.5)
    cmp_w2_v = nrm(ks[18], (DEPTH, CMP_HIDDEN, NSA_HEAD_DIM), CMP_HIDDEN ** -0.5)
    nsa_norm_g = 1.0 + nrm(ks[19], (DEPTH, NSA_HEAD_DIM), 0.02)
    mix_w_out = nrm(ks[20], (DEPTH, MIX_WIDTH, D_MODEL), MIX_WIDTH ** -0.5)
    final_norm_g = 1.0 + nrm(ks[21], (D_MODEL,), 0.02)
    return {"x": x, "c": c, "positions": positions, "ada_w": ada_w, "ada_b": ada_b,
            "norm_g": norm_g, "ffn_w_in": ffn_w_in, "ffn_w_out": ffn_w_out,
            "mix_w_in": mix_w_in, "gdn_conv_w": gdn_conv_w, "gdn_a_log": gdn_a_log,
            "gdn_dt_bias": gdn_dt_bias, "gdn_norm_g": gdn_norm_g,
            "cmp_pe_k": cmp_pe_k, "cmp_w1_k": cmp_w1_k, "cmp_w2_k": cmp_w2_k,
            "cmp_pe_v": cmp_pe_v, "cmp_w1_v": cmp_w1_v, "cmp_w2_v": cmp_w2_v,
            "nsa_norm_g": nsa_norm_g, "mix_w_out": mix_w_out, "final_norm_g": final_norm_g}

def first_block(x, c, positions, ada_w, ada_b, norm_g, ffn_w_in, ffn_w_out, mix_w_in,
              gdn_conv_w, gdn_a_log, gdn_dt_bias, gdn_norm_g, cmp_pe_k, cmp_w1_k, cmp_w2_k,
              cmp_pe_v, cmp_w1_v, cmp_w2_v, nsa_norm_g, mix_w_out, final_norm_g):
    B, T, D = x.shape
    half = ROT_DIM // 2
    inv_freq = jnp.power(ROPE_THETA, -jnp.arange(half, dtype=jnp.float32) * (2.0 / ROT_DIM))
    ang = positions.astype(jnp.float32)[..., None] * inv_freq
    cos = jnp.cos(ang)[:, :, None, :]
    sin = jnp.sin(ang)[:, :, None, :]
    cond = jax.nn.silu(c.astype(jnp.float32))
    for l in range(DEPTH):
        mod = (cond @ ada_w[l].astype(jnp.float32) + ada_b[l].astype(jnp.float32)).reshape(B, 3, 3, D).astype(x.dtype)
        h = modulate(rms_norm(x, norm_g[l, 0]), mod[:, 0, 0], mod[:, 0, 1])
        x = x + 0.5 * mod[:, 0, 2][:, None, :] * swiglu(h, ffn_w_in[l, 0], ffn_w_out[l, 0])
        h = modulate(rms_norm(x, norm_g[l, 1]), mod[:, 1, 0], mod[:, 1, 1])
        y = token_mix(h, mix_w_in[l], gdn_conv_w[l], gdn_a_log[l], gdn_dt_bias[l], gdn_norm_g[l],
                      cmp_pe_k[l], cmp_w1_k[l], cmp_w2_k[l], cmp_pe_v[l], cmp_w1_v[l], cmp_w2_v[l],
                      nsa_norm_g[l], mix_w_out[l], cos, sin)
        x = x + mod[:, 1, 2][:, None, :] * y.astype(x.dtype)
        h = modulate(rms_norm(x, norm_g[l, 2]), mod[:, 2, 0], mod[:, 2, 1])
        x = x + 0.5 * mod[:, 2, 2][:, None, :] * swiglu(h, ffn_w_in[l, 1], ffn_w_out[l, 1])
    return rms_norm(x, final_norm_g)


N_MIXERS = 2
N_META = 16
BLOCK = 128
EPS = 1e-6
NEG_INF = -1e30

FOX_HEADS = 16
FOX_HEAD_DIM = D_MODEL // FOX_HEADS
FOX_IN = 3 * D_MODEL + FOX_HEADS
FOX_FORGET_BIAS = 2.0

HG_HEADS = 8
HG_KEY_DIM = 128
HG_VAL_DIM = D_MODEL // HG_HEADS
HG_KEY_TOTAL = HG_HEADS * HG_KEY_DIM
HG_IN = 2 * HG_KEY_TOTAL + 2 * D_MODEL

N_GROUPS = 4
EXPERTS_PER_GROUP = 8
N_EXPERTS = N_GROUPS * EXPERTS_PER_GROUP
TOP_K = 2
D_EXPERT = D_MODEL // 2
EXPERT_ROW_BLOCK = 128


def rms_norm_2(x, gain):
    xf = x.astype(jnp.float32)
    y = xf * lax.rsqrt(jnp.mean(xf * xf, axis=-1, keepdims=True) + EPS)
    return (y * gain.astype(jnp.float32)).astype(x.dtype)

def front_pad(t, pad):
    widths = [(0, 0)] * t.ndim
    widths[1] = (pad, 0)
    return jnp.pad(t, widths)

def fox_attention(h, w_in, b_f, g_q, g_k, w_out):
    bsz, length, _ = h.shape
    q, k, v, f_logit = jnp.split(h @ w_in, [D_MODEL, 2 * D_MODEL, 3 * D_MODEL], axis=-1)
    q = rms_norm_2(q.reshape(bsz, length, FOX_HEADS, FOX_HEAD_DIM), g_q)
    k = rms_norm_2(k.reshape(bsz, length, FOX_HEADS, FOX_HEAD_DIM), g_k)
    v = v.reshape(bsz, length, FOX_HEADS, FOX_HEAD_DIM)
    log_f = jax.nn.log_sigmoid(f_logit.astype(jnp.float32) + b_f.astype(jnp.float32))
    pad = (-length) % BLOCK
    q, k, v, log_f = (front_pad(t, pad) for t in (q, k, v, log_f))
    lp = length + pad
    n_blk = lp // BLOCK
    cum = jnp.cumsum(log_f, axis=1).transpose(0, 2, 1)
    kh = k.transpose(0, 2, 1, 3)
    vh = v.transpose(0, 2, 1, 3)
    qb = q.reshape(bsz, n_blk, BLOCK, FOX_HEADS, FOX_HEAD_DIM).transpose(1, 0, 3, 2, 4)
    cb = cum.reshape(bsz, FOX_HEADS, n_blk, BLOCK).transpose(2, 0, 1, 3)
    key_pos = jnp.arange(lp)
    key_ok = key_pos >= pad
    scale = FOX_HEAD_DIM ** -0.5

    def attend(args):
        qi, ci, bi = args
        s = jnp.einsum('bhqd,bhkd->bhqk', qi, kh).astype(jnp.float32) * scale
        s = s + ci[..., :, None] - cum[:, :, None, :]
        q_pos = bi * BLOCK + jnp.arange(BLOCK)
        mask = (key_pos[None, :] <= q_pos[:, None]) & key_ok[None, :]
        p = jax.nn.softmax(jnp.where(mask, s, NEG_INF), axis=-1)
        return jnp.einsum('bhqk,bhkd->bhqd', p.astype(vh.dtype), vh)

    o = lax.map(attend, (qb, cb, jnp.arange(n_blk)))
    o = o.transpose(1, 0, 3, 2, 4).reshape(bsz, lp, D_MODEL)[:, pad:]
    return o @ w_out

def hgrn_lower_bounds(lb_logits):
    p = jax.nn.softmax(lb_logits.astype(jnp.float32), axis=0)
    cum = jnp.cumsum(p, axis=0)
    return cum - cum[:1]

def hgrn2_recurrence(h, w_in, b_f, lower_bound, g_o, w_out):
    bsz, length, _ = h.shape
    q, f_logit, v, g = jnp.split(
        h @ w_in, [HG_KEY_TOTAL, 2 * HG_KEY_TOTAL, 2 * HG_KEY_TOTAL + D_MODEL], axis=-1)
    f = lower_bound + (1.0 - lower_bound) * jax.nn.sigmoid(
        f_logit.astype(jnp.float32) + b_f.astype(jnp.float32))
    log_f = jnp.log(f)
    k = 1.0 - f
    q = jax.nn.silu(q.astype(jnp.float32))
    v = v.astype(jnp.float32)
    pad = (-length) % BLOCK
    lp = length + pad
    n_chk = lp // BLOCK

    def to_chunks(t, d):
        t = front_pad(t, pad).reshape(bsz, n_chk, BLOCK, HG_HEADS, d)
        return t.transpose(1, 0, 3, 2, 4)

    qc = to_chunks(q, HG_KEY_DIM)
    kc = to_chunks(k, HG_KEY_DIM)
    vc = to_chunks(v, HG_VAL_DIM)
    lc = to_chunks(log_f, HG_KEY_DIM)
    causal = jnp.tril(jnp.ones((BLOCK, BLOCK), dtype=bool))

    def step(state, args):
        qi, ki, vi, li = args
        b = jnp.cumsum(li, axis=2)
        o_inter = jnp.einsum('bhtk,bhkv->bhtv', qi * jnp.exp(b), state)
        diff = b[:, :, :, None, :] - b[:, :, None, :, :]
        decay = jnp.exp(jnp.where(causal[:, :, None], diff, -jnp.inf))
        scores = jnp.einsum('bhtk,bhsk,bhtsk->bhts', qi, ki, decay)
        o_intra = jnp.einsum('bhts,bhsv->bhtv', scores, vi)
        b_end = b[:, :, -1:, :]
        state = (jnp.exp(b_end[:, :, 0, :])[..., None] * state
                 + jnp.einsum('bhsk,bhsv->bhkv', ki * jnp.exp(b_end - b), vi))
        return state, o_inter + o_intra

    s0 = jnp.zeros((bsz, HG_HEADS, HG_KEY_DIM, HG_VAL_DIM), jnp.float32)
    _, o = lax.scan(step, s0, (qc, kc, vc, lc))
    o = o.transpose(1, 0, 3, 2, 4).reshape(bsz, lp, HG_HEADS, HG_VAL_DIM)[:, pad:]
    o = rms_norm_2(o, g_o).reshape(bsz, length, D_MODEL) * jax.nn.silu(g.astype(jnp.float32))
    return o.astype(h.dtype) @ w_out

def hier_moe(h, w_grp, b_grp, w_rt, b_rt, w_up, w_down):
    bsz, length, dm = h.shape
    n_tok = bsz * length
    n_asg = n_tok * TOP_K
    xt = h.reshape(n_tok, dm)
    g_prob = jax.nn.softmax((xt @ w_grp).astype(jnp.float32) + b_grp.astype(jnp.float32), axis=-1)
    g_gate, g_idx = lax.top_k(g_prob, 1)
    e_logit = ((xt @ w_rt).astype(jnp.float32) + b_rt.astype(jnp.float32)).reshape(
        n_tok, N_GROUPS, EXPERTS_PER_GROUP)
    e_logit = jnp.take_along_axis(e_logit, g_idx[:, :, None], axis=1)[:, 0]
    e_val, e_idx = lax.top_k(e_logit, TOP_K)
    gate = jax.nn.softmax(e_val, axis=-1) * g_gate
    expert = (g_idx * EXPERTS_PER_GROUP + e_idx).reshape(-1)
    order = jnp.argsort(expert)
    se = expert[order]
    tok = order // TOP_K
    w_sorted = gate.reshape(-1)[order]
    counts = jnp.bincount(expert, length=N_EXPERTS)
    padded = (counts + EXPERT_ROW_BLOCK - 1) // EXPERT_ROW_BLOCK * EXPERT_ROW_BLOCK
    start = jnp.cumsum(counts) - counts
    pend = jnp.cumsum(padded)
    pstart = pend - padded
    dest = pstart[se] + jnp.arange(n_asg) - start[se]
    n_blocks = (n_asg + N_EXPERTS * (EXPERT_ROW_BLOCK - 1) + EXPERT_ROW_BLOCK - 1) // EXPERT_ROW_BLOCK
    rows = n_blocks * EXPERT_ROW_BLOCK
    x_pad = jnp.zeros((rows, dm), h.dtype).at[dest].set(xt[tok])
    block_expert = jnp.minimum(
        jnp.searchsorted(pend, jnp.arange(n_blocks) * EXPERT_ROW_BLOCK, side='right'), N_EXPERTS - 1)

    def expert_block(args):
        xb, e = args
        gate_up = xb @ w_up[e]
        a, u = jnp.split(gate_up, 2, axis=-1)
        return (jax.nn.silu(a) * u) @ w_down[e]

    y_pad = lax.map(expert_block, (x_pad.reshape(n_blocks, EXPERT_ROW_BLOCK, dm), block_expert))
    y = y_pad.reshape(rows, dm)[dest] * w_sorted[:, None].astype(h.dtype)
    return jnp.zeros_like(xt).at[tok].add(y).reshape(bsz, length, dm)

def second_inputs(seed: int = 0) -> dict:
    key = jax.random.key(seed)
    ks = jax.random.split(key, 24)
    n_fox = (DEPTH + N_MIXERS - 1) // N_MIXERS
    n_hg = DEPTH // N_MIXERS
    out_scale = (2 * DEPTH) ** -0.5

    def nrm(k, shape, scale):
        return jax.random.normal(k, shape, jnp.float32) * scale

    def gain(k, shape):
        return 1.0 + nrm(k, shape, 0.02)

    return {
        'x': nrm(ks[0], (BATCH, SEQ, D_MODEL), 1.0),
        'meta_tokens': nrm(ks[1], (N_META, D_MODEL), 1.0),
        'fox_norm': gain(ks[2], (n_fox, D_MODEL)),
        'fox_w_in': nrm(ks[3], (n_fox, D_MODEL, FOX_IN), D_MODEL ** -0.5),
        'fox_b_f': FOX_FORGET_BIAS + nrm(ks[4], (n_fox, FOX_HEADS), 0.1),
        'fox_q_norm': gain(ks[5], (n_fox, FOX_HEAD_DIM)),
        'fox_k_norm': gain(ks[6], (n_fox, FOX_HEAD_DIM)),
        'fox_w_out': nrm(ks[7], (n_fox, D_MODEL, D_MODEL), D_MODEL ** -0.5 * out_scale),
        'hg_norm': gain(ks[8], (n_hg, D_MODEL)),
        'hg_w_in': nrm(ks[9], (n_hg, D_MODEL, HG_IN), D_MODEL ** -0.5),
        'hg_b_f': nrm(ks[10], (n_hg, HG_KEY_TOTAL), 0.02),
        'hg_lb_logits': nrm(ks[11], (DEPTH, HG_KEY_TOTAL), 0.5),
        'hg_o_norm': gain(ks[12], (n_hg, HG_VAL_DIM)),
        'hg_w_out': nrm(ks[13], (n_hg, D_MODEL, D_MODEL), D_MODEL ** -0.5 * out_scale),
        'moe_norm': gain(ks[14], (DEPTH, D_MODEL)),
        'moe_w_grp': nrm(ks[15], (DEPTH, D_MODEL, N_GROUPS), D_MODEL ** -0.5),
        'moe_b_grp': nrm(ks[16], (DEPTH, N_GROUPS), 0.01),
        'moe_w_rt': nrm(ks[17], (DEPTH, D_MODEL, N_EXPERTS), D_MODEL ** -0.5),
        'moe_b_rt': nrm(ks[18], (DEPTH, N_EXPERTS), 0.01),
        'moe_w_up': nrm(ks[19], (DEPTH, N_EXPERTS, D_MODEL, 2 * D_EXPERT), D_MODEL ** -0.5),
        'moe_w_down': nrm(ks[20], (DEPTH, N_EXPERTS, D_EXPERT, D_MODEL), D_EXPERT ** -0.5 * out_scale),
    }

def second_block(x, meta_tokens, fox_norm, fox_w_in, fox_b_f, fox_q_norm, fox_k_norm, fox_w_out,
              hg_norm, hg_w_in, hg_b_f, hg_lb_logits, hg_o_norm, hg_w_out,
              moe_norm, moe_w_grp, moe_b_grp, moe_w_rt, moe_b_rt, moe_w_up, moe_w_down):
    bsz = x.shape[0]
    meta = jnp.broadcast_to(meta_tokens[None].astype(x.dtype), (bsz, N_META, D_MODEL))
    h = jnp.concatenate([meta, x], axis=1)
    lower_bounds = hgrn_lower_bounds(hg_lb_logits)
    for i in range(DEPTH):
        j = i // N_MIXERS
        if i % N_MIXERS == 0:
            h = h + fox_attention(rms_norm_2(h, fox_norm[j]), fox_w_in[j], fox_b_f[j],
                                  fox_q_norm[j], fox_k_norm[j], fox_w_out[j])
        else:
            h = h + hgrn2_recurrence(rms_norm_2(h, hg_norm[j]), hg_w_in[j], hg_b_f[j],
                                     lower_bounds[i], hg_o_norm[j], hg_w_out[j])
        h = h + hier_moe(rms_norm_2(h, moe_norm[i]), moe_w_grp[i], moe_b_grp[i],
                         moe_w_rt[i], moe_b_rt[i], moe_w_up[i], moe_w_down[i])
    return h[:, N_META:]


def setup_inputs(seed=0):
    out = dict(first_inputs(seed))
    for name, value in second_inputs(seed + 1).items():
        if name != "x":
            out[name + "_2"] = value
    return out


def reference(
    x, c, positions, ada_w, ada_b, norm_g, ffn_w_in, ffn_w_out, mix_w_in, gdn_conv_w, gdn_a_log,
    gdn_dt_bias, gdn_norm_g, cmp_pe_k, cmp_w1_k, cmp_w2_k, cmp_pe_v, cmp_w1_v, cmp_w2_v,
    nsa_norm_g, mix_w_out, final_norm_g, meta_tokens_2, fox_norm_2, fox_w_in_2, fox_b_f_2,
    fox_q_norm_2, fox_k_norm_2, fox_w_out_2, hg_norm_2, hg_w_in_2, hg_b_f_2, hg_lb_logits_2,
    hg_o_norm_2, hg_w_out_2, moe_norm_2, moe_w_grp_2, moe_b_grp_2, moe_w_rt_2, moe_b_rt_2,
    moe_w_up_2, moe_w_down_2,
):
    x = first_block(
        x, c, positions, ada_w, ada_b, norm_g, ffn_w_in, ffn_w_out, mix_w_in, gdn_conv_w,
        gdn_a_log, gdn_dt_bias, gdn_norm_g, cmp_pe_k, cmp_w1_k, cmp_w2_k, cmp_pe_v, cmp_w1_v,
        cmp_w2_v, nsa_norm_g, mix_w_out, final_norm_g,
    )
    return second_block(
        x, meta_tokens_2, fox_norm_2, fox_w_in_2, fox_b_f_2, fox_q_norm_2, fox_k_norm_2,
        fox_w_out_2, hg_norm_2, hg_w_in_2, hg_b_f_2, hg_lb_logits_2, hg_o_norm_2, hg_w_out_2,
        moe_norm_2, moe_w_grp_2, moe_b_grp_2, moe_w_rt_2, moe_b_rt_2, moe_w_up_2, moe_w_down_2,
    )


_drawn_inputs = setup_inputs


def setup_inputs(seed=0):
    import zlib

    import numpy as np

    out = dict(_drawn_inputs(seed))
    spreads = {}
    factors = {'norm_g': 2.789,
     'gdn_norm_g': 5.031,
     'cmp_pe_k': 4.696,
     'nsa_norm_g': 4.081,
     'fox_norm_2': 3.613,
     'fox_b_f_2': 2.75,
     'fox_q_norm_2': 4.021,
     'fox_k_norm_2': 7.068,
     'hg_norm_2': 3.996,
     'hg_b_f_2': 64.0,
     'hg_lb_logits_2': 2.976,
     'hg_o_norm_2': 14.468,
     'moe_b_grp_2': 23.765,
     'moe_b_rt_2': 16.221,
     'moe_norm_2': 6.003}
    for name, (base, spread) in spreads.items():
        noise = np.random.default_rng([zlib.crc32(name.encode()), seed]).standard_normal(out[name].shape)
        drawn = base * np.exp(spread * noise) if base else spread * noise
        out[name] = jnp.asarray(drawn.astype(out[name].dtype))
    for name, factor in factors.items():
        out[name] = (out[name] * factor).astype(out[name].dtype)
    return out
```

```python
from contextlib import ExitStack

import numpy as np
import concourse.bass as bass
from concourse import mybir

P = 128
D = 1024
KC = D // P
T1 = 256
META = 16
T2 = T1 + META
DEPTH = 2
NADA = 9 * D // P
GH = 4
F = 2816
STEP = 256
NE = 32
W = 64
SLOTS = 2 * T2
GROUPS, PER_GROUP = 4, 8
FOXH, FOXD = 16, 64
HGH = 8
NCMP = 15
ROT = 16
LEVELS = 7
RING = 8
COLS = 256
SLAB = KC * COLS
NEG = -1e30
KT2 = ((0, META), (META, P), (META + P, P))
KT1 = ((0, P), (P, P))

F32 = mybir.dt.float32
F32R = mybir.dt.float32r
HI_RING = 6
I32 = mybir.dt.int32
U32 = mybir.dt.uint32
ALU = mybir.AluOpType
ACT = mybir.ActivationFunctionType
X_AXIS = mybir.AxisListType.X


def layout(items):
    at, out = 0, {}
    for name, width in items:
        out[name] = (at, width)
        at += width
    return out, at


CONST, NCONST = layout([("ident", P), ("ones", P), ("upper", P), ("negrow", T2), ("strict", P), ("blk64", P),
                        ("rope", P), ("lev", LEVELS * P), ("levT", LEVELS * P), ("cneg", 2 * NCMP),
                        ("invf", 1), ("eps", 1), ("iota", SLOTS)])
VEC, NVEC = layout([("c", KC), ("ada_b", DEPTH * NADA), ("norm_g", DEPTH * 3 * KC), ("final_g", KC),
                    ("conv", DEPTH * 4 * 12), ("gdn_g", DEPTH), ("nsa_g", DEPTH), ("fox_g", KC), ("qg", 1),
                    ("kg", 1), ("hg_g", KC), ("hg_bf", KC), ("hg_lb", 2 * KC), ("hg_og", 1),
                    ("moe_g", 2 * KC), ("a_log", DEPTH * GH), ("dt", DEPTH * GH), ("moe_b", DEPTH * 36),
                    ("fox_bf_row", FOXH), ("w2k", DEPTH * 64), ("w2v", DEPTH * 64), ("pek", DEPTH * 16),
                    ("pev", DEPTH * 16), ("wf", KC * FOXH), ("wr", DEPTH * KC * 36)])


def stage_list():
    out = [("ada", 0, 0, ADA_PART)]
    for l in range(DEPTH):
        out += [("ffn", l, 0), ("mix", l), ("ffn", l, 1)]
    return out + [("final",), ("fox",), ("moe", 0), ("hg",), ("moe", 1)]


ADA_PART = KC * 3 * P // COLS


def ada_share(l, i, step):
    for at, layer, first in (((0, 0), 0, ADA_PART), ((0, 1), 1, 0), ((1, 0), 1, ADA_PART)):
        if (l, i) == at:
            return layer, first + step, first + step + 1 + (step == FFN_STEPS - 1)
    return 0, 0, 0


FFN_STEPS = F // STEP


def slab_plan(stages):
    out = []
    for st in stages:
        if st[0] == "ada":
            out += [("ada", st[1], s, "dve") for s in range(st[2], st[3])]
        elif st[0] == "ffn":
            out += [("gate", st[1], st[2], 0, "pe"), ("up", st[1], st[2], 0, "pe")]
            for s in range(FFN_STEPS):
                if s + 1 < FFN_STEPS:
                    out += [("gate", st[1], st[2], s + 1, "pe"), ("up", st[1], st[2], s + 1, "pe")]
                out += [("down", st[1], st[2], s, "pe")]
                layer, lo, hi = ada_share(st[1], st[2], s)
                out += [("ada", layer, i, "dve") for i in range(lo, hi)]
        elif st[0] == "mix":
            for s in range(14):
                out += [("mixin", st[1], s, "pe")]
                out += [("ada", st[1], 2 * ADA_PART + s, "dve")] if s < ADA_PART else []
            out += [("cmpw", st[1], s, "pe") for s in range(2)]
            out += [("mixout", st[1], s, "pe") for s in range(4)]
        elif st[0] == "fox":
            out += [("foxin", s, "pe") for s in range(12)] + [("foxout", s, "pe") for s in range(4)]
        elif st[0] == "hg":
            out += [("hgin", s, "pe") for s in range(16)] + [("hgout", s, "pe") for s in range(4)]
        elif st[0] == "moe":
            steps = [(e, h) for e in range(NE) for h in range(2)]
            out += [("egate", st[1], *steps[0], "pe"), ("eup", st[1], *steps[0], "pe")]
            for s in range(len(steps)):
                if s + 1 < len(steps):
                    out += [("egate", st[1], *steps[s + 1], "pe"), ("eup", st[1], *steps[s + 1], "pe")]
                out += [("edown", st[1], *steps[s], "pe")]
    return out


def nth_slab(st, slab, n):
    return slab + n + (min(n, ADA_PART) if st[0] == "mix" else 0)


def slab_width(s):
    return KC * 32 if s[0] == "mixin" and s[2] == 13 else SLAB


def releases(plan):
    count = dict(up_done=0, y_done=0, ada_acc=0, proj_done=0)
    out = []
    for s in plan:
        if s[0] in ("gate", "egate"):
            out.append(("up_done", count["up_done"] + 2))
            continue
        if s[0] in ("up", "eup"):
            name, n = "up_done", 2
        elif s[0] in ("down", "edown"):
            name, n = "y_done", KC
        elif s[0] == "ada":
            name, n = "ada_acc", 1
        else:
            name, n = "proj_done", slab_jobs(s)
        count[name] += n
        out.append((name, count[name]))
    return out


def slab_jobs(s):
    return {"mixin": (2,) * 11 + (3, 3, 2), "cmpw": (1, 1), "foxin": (2,) * 8 + (3,) * 4,
            "hgin": (2,) * 8 + (3,) * 4 + (2,) * 4}.get(s[0], (2,) * 4)[s[-2]]


def stage_jobs(st):
    out = []
    if st[0] == "mix":
        out += [("qkv", c, c // 2, c % 2 * P, "act") for c in range(12)]
        out += [("z", c, 6 + c // 2, c % 2 * P, "act") for c in range(4)]
        out += [("nq", c, 8 + c // 2, c % 2 * P, "act") for c in range(4)]
        out += [("nk", 0, 10, 0, "act"), ("vc", 0, 10, P, "act")]
        for i, slab in ((1, 11), (2, 12)):
            out += [("nk", i, slab, 0, "act")] + [("vtok", (i - 1, t), slab, P, "dve") for t in range(2)]
        out += [("gba", t, 13, 0, "dve") for t in range(2)]
        out += [("cmp", c, 14 + c, 0, "act") for c in range(2)]
        out += [("out", c, 16 + c // 2, c % 2 * P, "dve") for c in range(KC)]
    elif st[0] == "fox":
        out += [("fq", c, c // 2, c % 2 * P, "dve") for c in range(2 * KC)]
        out += [("fv", (i, t), 8 + i, 0, "act") for i in range(4) for t in range(3)]
        out += [("out", c, 12 + c // 2, c % 2 * P, "dve") for c in range(KC)]
    elif st[0] == "hg":
        out += [("hq", c, c // 2, c % 2 * P, "act") for c in range(2 * KC)]
        out += [("hv", (i, t), 8 + i, 0, "act") for i in range(4) for t in range(3)]
        out += [("hgate", c, 12 + c // 2, c % 2 * P, "act") for c in range(KC)]
        out += [("out", c, 16 + c // 2, c % 2 * P, "dve") for c in range(KC)]
    return out


def job_table(stages):
    jobs, read, n = [], [], {"act": 0, "dve": 0}
    for st in stages:
        for j in stage_jobs(st):
            n[j[4]] += 1
            jobs.append(j)
            read.append(("proj_" + j[4], n[j[4]]))
    return jobs, read


def x_written(stages):
    out, steps, jobs, dve_jobs, h = [("x_in", 32)], 0, 0, 0, 0
    for st in stages:
        h += KC if st[0] != "ada" else 0
        if st[0] in ("ffn", "moe"):
            steps += FFN_STEPS if st[0] == "ffn" else 2 * NE
            out.append(("y_added", KC * steps))
        elif st[0] in ("mix", "fox", "hg"):
            dve_jobs += sum(j[4] == "dve" for j in stage_jobs(st))
            out.append(("proj_dve", dve_jobs))
        elif st[0] == "final":
            out.append(("h_mul", h))
        else:
            out.append(out[-1])
    return out


def rows(w, n):
    return np.ascontiguousarray(w.reshape(n, P, -1).transpose(1, 0, 2)).reshape(P, -1)


def nsa_heads():
    return np.concatenate([np.arange((g * 4 + j) * 64, (g * 4 + j) * 64 + 64) for j in range(4) for g in range(2)])


def slab_array(s, a):
    k = s[0]
    part = lambda w, i, at=0: rows(w[:, at + i * COLS:at + (i + 1) * COLS], KC)
    if k == "ada":
        return part(a["ada_w"][s[1]], s[2])
    if k in ("gate", "up"):
        return part(a["ffn_w_in"][s[1], s[2]], s[3], F if k == "up" else 0)
    if k == "down":
        return rows(a["ffn_w_out"][s[1], s[2]][s[3] * STEP:(s[3] + 1) * STEP], STEP // P)
    if k == "mixin":
        w = a["mix_w_in"][s[1]]
        if s[2] < 8:
            return part(w, s[2])
        if s[2] < 10:
            return part(w[:, 2056 + nsa_heads()], s[2] - 8)
        if s[2] < 13:
            return part(w, s[2] - 10, 2568)
        return rows(np.concatenate([w[:, 3336:3360], w[:, 2048:2056]], axis=1), KC)
    if k == "cmpw":
        return rows(a["cmp_w1_v" if s[2] else "cmp_w1_k"][s[1]], 16)
    if k == "mixout":
        w = a["mix_w_out"][s[1]]
        return part(np.concatenate([w[:512], w[512 + nsa_heads()]], axis=0), s[2])
    if k in ("foxin", "foxout", "hgin", "hgout"):
        name = {"foxin": "fox_w_in_2", "foxout": "fox_w_out_2", "hgin": "hg_w_in_2", "hgout": "hg_w_out_2"}[k]
        return part(a[name][0], s[1])
    if k in ("egate", "eup"):
        return part(a["moe_w_up_2"][s[1], s[2]], s[3], 512 if k == "eup" else 0)
    return rows(a["moe_w_down_2"][s[1], s[2]][s[3] * STEP:(s[3] + 1) * STEP], STEP // P)


def cols(v, n):
    return np.ascontiguousarray(v.reshape(n, P).T)


def bcast(v):
    return np.broadcast_to(v.reshape(1, -1), (P, v.size))


def vec_pack(a):
    two = lambda v: np.concatenate([v, v]).reshape(P, 1)
    conv = a["gdn_conv_w"].reshape(DEPTH * 4 * 12, P)
    parts = {
        "c": cols(a["c"][0], KC), "ada_b": cols(a["ada_b"], DEPTH * NADA), "norm_g": cols(a["norm_g"], DEPTH * 3 * KC),
        "final_g": cols(a["final_norm_g"], KC), "conv": conv.T, "gdn_g": a["gdn_norm_g"].T,
        "nsa_g": np.concatenate([two(a["nsa_norm_g"][l]) for l in range(DEPTH)], axis=1),
        "fox_g": cols(a["fox_norm_2"], KC), "qg": two(a["fox_q_norm_2"][0]), "kg": two(a["fox_k_norm_2"][0]),
        "hg_g": cols(a["hg_norm_2"], KC), "hg_bf": cols(a["hg_b_f_2"], KC), "hg_lb": cols(a["hg_lb_logits_2"], 2 * KC),
        "hg_og": a["hg_o_norm_2"].T, "moe_g": cols(a["moe_norm_2"], 2 * KC), "a_log": bcast(a["gdn_a_log"]),
        "dt": bcast(a["gdn_dt_bias"]),
        "moe_b": bcast(np.concatenate([a["moe_b_grp_2"], a["moe_b_rt_2"]], axis=1)),
        "fox_bf_row": bcast(a["fox_b_f_2"]),
        "w2k": np.concatenate(list(a["cmp_w2_k"]), axis=1), "w2v": np.concatenate(list(a["cmp_w2_v"]), axis=1),
        "pek": cols(a["cmp_pe_k"], DEPTH * 16), "pev": cols(a["cmp_pe_v"], DEPTH * 16),
        "wf": rows(a["fox_w_in_2"][0][:, 3 * D:], KC),
        "wr": np.concatenate([rows(np.concatenate([a["moe_w_grp_2"][l], a["moe_w_rt_2"][l]], axis=1), KC)
                              for l in range(DEPTH)], axis=1),
    }
    return np.ascontiguousarray(np.concatenate([parts[n] for n in VEC], axis=1))


def const_pack():
    r = np.arange(P)
    q, k = r[:, None], r[None, :]
    out = {"ident": np.eye(P), "ones": np.ones((P, P)), "upper": q <= k, "strict": k < q, "blk64": q // 64 == k // 64}
    out["negrow"] = np.concatenate([np.zeros((P, T2 - P)), np.where(k <= q, 0.0, NEG)], axis=1)
    rope = np.zeros((P, P))
    for p in range(P):
        if p % 64 < 8:
            rope[p + 8, p] = -1.0
        elif p % 64 < 16:
            rope[p - 8, p] = 1.0
    out["rope"] = rope
    lev = [((q // (2 * s) == k // (2 * s)) & (q % (2 * s) >= s) & (k % (2 * s) < s)).astype(float)
           for s in (2 ** i for i in range(LEVELS))]
    out["lev"] = np.concatenate(lev, axis=1)
    out["levT"] = np.concatenate([m.T for m in lev], axis=1)
    out["cneg"] = np.concatenate([np.where(16 * np.arange(NCMP)[None] + 31 <= t0 + q, 0.0, NEG) for t0, _ in KT1], axis=1)
    d = r % 64
    inv = np.power(np.float32(500000.0), -(d % 8).astype(np.float32) * np.float32(2.0 / ROT))
    out["invf"] = np.where(d < ROT, inv, 0.0)[:, None]
    out["eps"] = np.full((P, 1), 1e-6)
    out["iota"] = np.broadcast_to(np.arange(SLOTS)[None], (P, SLOTS))
    return np.ascontiguousarray(np.concatenate([np.asarray(out[n], np.float32) for n in CONST], axis=1))


def host_arrays(a, stages):
    plan = slab_plan(stages)
    slabs = np.zeros((len(plan), P, SLAB), np.float32)
    for i, s in enumerate(plan):
        v = slab_array(s, a)
        slabs[i, :, :v.shape[1]] = v
    return {
        "slabs": slabs, "vec": vec_pack(a), "const": const_pack(),
        "xT": rows(np.ascontiguousarray(a["x"][0].T), KC),
        "metaT": rows(np.ascontiguousarray(a["meta_tokens_2"].T), KC),
        "pos": np.ascontiguousarray(np.broadcast_to(a["positions"], (P, T1))),
    }


class Marks:

    def __init__(self, noted=None):
        self.noted = noted
        self.seen = {}

    def put(self, engine, key):
        seen = self.seen.setdefault(engine, {})
        assert key not in seen, key
        seen[key] = len(seen) + 1

    def value(self, engine, key):
        return self.noted[engine][key] if self.noted else 1


def build(nc, ap, stages, marks):
    plan = slab_plan(stages)
    free = releases(plan)
    with ExitStack() as ctx:
        sb = lambda name, shape, dt=F32: ctx.enter_context(nc.sbuf_tensor(name, shape, dt))
        sem = lambda name: ctx.enter_context(nc.semaphore(name))

        def twice(name, shape):
            with nc.sbuf_tensor(name, shape, F32) as plain:
                pass
            return plain, sb(name + "_parts", shape, F32R)
        ring, ring_parts = twice("ring", [P, RING, SLAB])
        x = sb("x", [P, KC, T2])
        h = sb("h", [P, KC, T2])
        sq = sb("sq", [P, KC, T2])
        hid = sb("hid", [P, 2, 2, T2])
        sil = sb("sil", [P, 2, T2])
        const = sb("constants", [P, NCONST])
        vec = sb("vectors", [P, NVEC])
        cos = sb("cos", [P, T1])
        sin = sb("sin", [P, T1])
        mod = sb("mod", [P, DEPTH, NADA])
        cond = sb("cond", [P, KC])
        rstd = sb("rstd", [P, T2])
        acc = sb("acc", [P, 4, COLS])
        arena, arena_parts = twice("arena", [P, 21640])
        ps = ctx.enter_context(nc.psum_tensor("ps", [P, 8, 512], F32))
        col = lambda name, i=0, n=1: vec[:, VEC[name][0] + i:VEC[name][0] + i + n]
        cst = lambda name, i=0, n=P: const[:, CONST[name][0] + i:CONST[name][0] + i + n]
        ident, ones, upper = cst("ident"), cst("ones"), cst("upper")
        eps = cst("eps", 0, 1)

        def view(at, *shape, whole=arena):
            n = int(np.prod(shape))
            v = whole[:, at:at + n]
            if len(shape) == 1:
                return v
            names = "abcd"[:len(shape)]
            return v.rearrange(f"p ({' '.join(names)}) -> p {' '.join(names)}", **dict(zip(names, shape)))

        s = {n: sem(n) for n in (
            "consts", "x_in", "pos_in", "cond_ready", "table_ready", "act_chain", "dve_chain", "pool_chain",
            "sq_ready", "ss_ready", "rstd_ready", "h_mul", "h_ready", "ada_acc", "ada_chain", "ada_col", "w_hi", "w_lo",
            "h_hi", "h_lo",
            "up_done", "silu_done", "hid_done", "y_done", "y_added", "proj_done", "proj_act",
            "proj_dve", "ada_ps", "rope_ready", "out_done", "pe_step", "act_step", "dve_step",
            *(f"{n}{l}" for l in range(2) for n in ("gb_in", "gb_ps", "gb_ready", "gated", "xe_ready",
                                                    "sparse_pe", "sparse_act", "sparse_dve")))}
        slot_loaded = [sem(f"slot{i}_loaded") for i in range(RING)]

        def slab_here(eng, i):
            eng.wait_ge(slot_loaded[i % RING], 16 * (i // RING + 1))

        def slab_view(i, k=KC):
            return ring[:, i % RING, :].rearrange("p (k n) -> p k n", k=k)

        def low_view(i, k=KC):
            return ring_parts[:, i % RING, :].rearrange("p (k n) -> p k n", k=k)

        split_slabs = [i for i, sl in enumerate(plan) if sl[0] in ("gate", "up", "down")]
        split_at = {i: m for m, i in enumerate(split_slabs)}


        block = ctx.enter_context(nc.Block())

        @block.sync
        def _(sp):
            sp.dma_start(vec[:], ap["vec"]).then_inc(s["consts"], 16)
            sp.dma_start(const[:], ap["const"]).then_inc(s["consts"], 16)
            sp.dma_start(x[:, :, META:T2], ap["xT"].rearrange("p (k n) -> p k n", k=KC)).then_inc(s["x_in"], 16)
            sp.dma_start(x[:, :, 0:META], ap["metaT"].rearrange("p (k n) -> p k n", k=KC)).then_inc(s["x_in"], 16)
            sp.dma_start(arena[:, 0:T1].bitcast(I32), ap["pos"]).then_inc(s["pos_in"], 16)

            def load(i):
                if i >= RING:
                    name, value = free[i - RING]
                    sp.wait_ge(s[name], value)
                w = slab_width(plan[i])
                sp.dma_start(ring[:, i % RING, 0:w], ap["slabs"][i, :, 0:w]).then_inc(slot_loaded[i % RING], 16)

            at, t = 0, 0
            for st in stages:
                if st[0] != "moe":
                    n = len(slab_plan([st]))
                    for i in range(at, at + n):
                        load(i)
                    at += n
                    t += FFN_STEPS if st[0] == "ffn" else 0
                    continue
                total, body = 3 * 2 * NE, 24
                trips = (total - 10) // body
                for i in range(at, at + 10):
                    load(i)
                with sp.Fori(0, trips) as it:
                    for k in range(body):
                        slot = (at + 10 + k) % RING
                        step, r = divmod(k, 3)
                        if r < 2:
                            sp.wait_ge(s["up_done"], it * 16 + 2 * (t + step + 2))
                        else:
                            sp.wait_ge(s["y_done"], it * (8 * KC) + KC * (t + step + 1))
                        src = ap["slabs"][bass.ds(it * body + (at + 10 + k), 1)].rearrange("o p c -> (o p) c")
                        sp.dma_start(ring[:, slot, :], src).then_inc(slot_loaded[slot], 16)
                for i in range(at + 10 + body * trips, at + total):
                    load(i)
                at += total
                t += 2 * NE
            name, value = x_written(stages)[-1]
            sp.wait_ge(s[name], value)
            sp.dma_start(ap["outT"].rearrange("p (k n) -> p k n", k=KC), x[:, :, META:T2]).then_inc(s["out_done"], 16)
            sp.wait_ge(s["out_done"], 16)

        def stepper(engine, l=None):
            eng = {"pe": nc.tensor, "act": nc.scalar, "dve": nc.vector}[engine]
            name = (lambda e: e + "_step") if l is None else (lambda e: f"sparse_{e}{l}")

            def mark(ins, *key):
                marks.put(name(engine), key)
                ins.then_inc(s[name(engine)], 1)

            def await_(other, *key):
                eng.wait_ge(s[name(other)], marks.value(name(other), key))
            return mark, await_

        jobs, job_read = job_table(stages)
        written = x_written(stages)
        bank = lambda i, n=512: ps[:, i, 0:n]
        xs = lambda n: x[:, :, T2 - n:T2]

        QI, QO, ZS, NQK, VC, KC2, VT, SMALL = 0, 3108, 6180, 7204, 8996, 9252, 10276, 10788
        UU, PPP, LO = 0, 1024, 2048
        KCMP, HC, VCMP, CB = SMALL + 264, 11108, 11168, 11296
        VB, KBE, KD, DECT, LL, QE, TT, OT, NW, STATE, VN = (11300, 12324, 13348, 14372, 15396, 16420, 17444, 18468,
                                                           19492, 20004, 20516)
        ATT = DECT
        FQ, FK, FV, LF, CQ, NCUM = 0, 2176, 4352, 7424, 7568, 7616
        PB, PT, RTMP, STAT = (11300, 12388, 13924, 14500)
        OACC = 14600
        hid_v = view(VN, 8, P)

        job_at = [0]
        for st_ in stages:
            job_at.append(job_at[-1] + len(stage_jobs(st_)))
        proj_end = lambda q: job_at[q] + 30
        def shares_of(st):
            if st[0] == "ffn":
                return (FFN_STEPS, ADA_PART) if ada_share(*st[1:], 0)[2] else (0, 0)
            return (1, ADA_PART) if st[0] in ("ada", "mix") else (0, 0)
        shares_before = lambda q: sum(shares_of(r)[0] for r in stages[:q])
        ada_before = lambda q: sum(shares_of(r)[1] for r in stages[:q])
        before = lambda q, e: sum(j[4] == e for j in jobs[:job_at[q]])
        act_before = lambda q: before(q, "act")
        dve_before = lambda q: before(q, "dve")
        fox_chunk = lambda c: view(FQ, 2 * KC, T2)[:, c]

        def attn_units(st):
            if st[0] == "fox":
                return [(0, i, j) for i in range(3) for j in range(KC)]
            return [(br, i, j) for br in range(3) for i in range(2) for j in range(4)]

        def attn_operands(st, br, i, j):
            if st[0] == "fox":
                vals = view(FV, 3, D)
                vv = [[(k0, kn, vals[0:kn, t, (2 * j + e) * 64:(2 * j + e) * 64 + 64])
                       for t, (k0, kn) in enumerate(KT2[:i + 1])] for e in range(2)]
                return view(FQ, KC, T2)[:, j], view(FK, KC, T2)[:, j], vv, KT2, sum(KT2[i])
            nqk = view(NQK, 7, T1)
            if br == 0:
                vv = [[(0, NCMP, view(VCMP, 2, 64)[0:NCMP, e])] for e in range(2)]
                return nqk[:, j], view(KCMP, NCMP), vv, KT1, NCMP
            vals = view(VT, 2, 2, P)
            vv = [[(k0, kn, vals[0:kn, br - 1, t, 64 * e:64 * e + 64]) for t, (k0, kn) in enumerate(KT1[:i + 1])]
                  for e in range(2)]
            return nqk[:, j], nqk[:, 4 + br], vv, KT1, sum(KT1[i])
        HQ, HB, HK, HG, HV = 0, 2176, 4352, 6528, 8704
        HSC, HE, HTMP, HQE, HKD, HKDT, HST, HO, HLB, HEB = (11776, 12800, 13824, 14848, 15872, 16896, 17920, 18944,
                                                             21120, 21160)
        RT, GT, GTT, GSEL, GBC = 0, 480, 576, 848, 1392
        MM, OH, POS, PRD, STARTS, CNT, INTS = 1936, 2032, 2224, 2320, 2512, 2544, 2580
        XE, PM, PW, PTMP, GP, HTOK, XS, YS, YT = 2620, 3644, 5276, 6908, 7452, 8812, 11884, 16748, 8812

        most_at = view(INTS, NE + 1).bitcast(I32)[0:1, NE:NE + 1]

        def expert_at(e, it):
            ints = view(INTS, NE + 1).bitcast(I32)
            return ints[0:1, e:e + 1] if it is None else ints[0:1, bass.ds(it * 4 + e, 1)]

        slab_at = [0]
        for st_ in stages:
            slab_at.append(slab_at[-1] + len(slab_plan([st_])))
        part = lambda at, *shape: view(at, *shape, whole=arena_parts)
        HI_W = 5 * T1
        HH_HI = HI_W + HI_RING * SLAB
        hh_hi, hh_lo = part(HH_HI, KC, T1), part(HH_HI + KC * T1, KC, T1)
        hid_hi, hid_lo = part(HH_HI + 2 * KC * T1, 2, 2, T1), part(HH_HI + (2 * KC + 4) * T1, 2, 2, T1)

        def hi_slab(i, k=KC):
            return part(HI_W + split_at[i] % HI_RING * SLAB, k, SLAB // k)

        def split_seq(q, st):
            return [i for i in split_slabs if slab_at[q] <= i < slab_at[q + 1]] if st[0] == "ffn" else []

        def norm_of(st):
            if st[0] == "ffn" or st[0] == "mix":
                l, i = st[1], (1 if st[0] == "mix" else 2 * st[2])
                m = lambda j: (lambda k: mod[:, l, (3 * i + j) * KC + k:(3 * i + j) * KC + k + 1])
                return T1, m(1), m(0)
            name, at = {"final": ("final_g", 0), "fox": ("fox_g", 0), "hg": ("hg_g", 0)}.get(st[0], ("moe_g", None))
            at = KC * st[1] if at is None else at
            return (T1 if st[0] == "final" else T2), (lambda k: col(name, at + k)), None

        def gate_col(l, i, k):
            return mod[:, l, (3 * i + 2) * KC + k:(3 * i + 2) * KC + k + 1]

        def by_pool(st, n):
            return st[0] == "ffn" or (st[0] == "ada" and n % 3 == 1)

        def sum_slab(eng, steps, i, n):
            slab_here(eng, i)
            if n >= 4:
                eng.wait_ge(s["ada_ps"], n - 3)
            wt = slab_view(i)
            for k in range(KC):
                if k == 0:
                    ins = nc.vector.tensor_scalar(acc[:, n % 4, :], wt[:, 0, :], cond[:, 0:1], None, ALU.mult)
                else:
                    if k == KC - 1 and n:
                        eng.wait_ge(s["ada_acc"], n)
                    ins = nc.vector.scalar_tensor_tensor(out=acc[:, n % 4, :], in0=wt[:, k, :], scalar=cond[:, k:k + 1],
                                                         in1=acc[:, n % 4, :], op0=ALU.mult, op1=ALU.add)
                if k < KC - 1:
                    steps[0] += 1
                    ins.then_inc(s["ada_chain"], 1)
                    eng.wait_ge(s["ada_chain"], steps[0])
            ins.then_inc(s["ada_acc"], 1)

        @block.gpsimd
        def _(pool):
            pool.wait_ge(s["cond_ready"], 1)
            n = done = 0
            for q, st in enumerate(stages):
                for i in range(slab_at[q], slab_at[q + 1]):
                    if plan[i][0] != "ada":
                        continue
                    if by_pool(st, n):
                        slab_here(pool, i)
                        wt = slab_view(i)
                        c = cond.rearrange("p (k n) -> p k n", n=1).to_broadcast([P, KC, COLS])
                        ins = nc.gpsimd.tensor_tensor(wt, wt, c, ALU.mult)
                        half = KC // 2
                        while half:
                            ins.then_inc(s["pool_chain"], 1)
                            done += 1
                            pool.wait_ge(s["pool_chain"], done)
                            if half > 1:
                                out = wt[:, 0:half]
                            else:
                                pool.wait_ge(s["ada_acc"], n)
                                if n >= 4:
                                    pool.wait_ge(s["ada_ps"], n - 3)
                                out = acc[:, n % 4:n % 4 + 1]
                            ins = nc.gpsimd.tensor_tensor(out, wt[:, 0:half], wt[:, half:2 * half], ALU.add)
                            half //= 2
                        ins.then_inc(s["ada_acc"], 1)
                    n += 1

        @block.tensor
        def _(pe):
            trip = [None]

            def w(name, value, per_trip):
                pe.wait_ge(s[name], value if trip[0] is None else trip[0] * per_trip + value)

            def slab_in(i):
                at = 16 * (i // RING + 1)
                pe.wait_ge(slot_loaded[i % RING], at if trip[0] is None else trip[0] * (24 // RING * 16) + at)

            mark, await_ = stepper("pe")

            def run_jobs(q, st, lo, hi, slab, job, rhs=h):
                n = T1 if st[0] == "mix" else T2
                seen = None
                for i, (kind, idx, sl, c0, _) in list(enumerate(stage_jobs(st)))[lo:hi]:
                    j = job + i
                    b = j % 4
                    if sl != seen:
                        if st[0] == "mix" and 3 <= sl < 14:
                            if sl == 3:
                                pe.wait_ge(s["ada_col"], shares_before(q))
                            ada_cols(ada_before(q) + sl - 3, sl - 3)
                        slab_here(pe, nth_slab(st, slab, sl))
                        seen = sl
                    if j >= 4:
                        pe.wait_ge(s[job_read[j - 4][0]], job_read[j - 4][1])
                    wt = slab_view(nth_slab(st, slab, sl))
                    if kind == "cmp":
                        wt, kc2 = slab_view(nth_slab(st, slab, sl), 16), view(KC2, 2, 2, T1)
                        pe_col = "pev" if idx else "pek"
                        for i2 in range(16):
                            nc.tensor.matmul(ps[:, b, 0:2 * NCMP], wt[:, i2, :], kc2[:, idx, :, 2 * i2:2 * i2 + 225:16],
                                             start=(i2 == 0), stop=(i2 == 15))
                        for i2 in range(16):
                            mm = nc.tensor.matmul(ps[:, b, 64:65], wt[:, i2, :], col(pe_col, st[1] * 16 + i2),
                                                  start=(i2 == 0), stop=(i2 == 15))
                    elif kind in ("vtok", "gba", "fv", "hv"):
                        t = idx if kind == "gba" else idx[1]
                        at, size = (KT1 if st[0] == "mix" else KT2)[t]
                        width = {"vtok": P, "gba": 32}.get(kind, COLS)
                        if kind == "gba":
                            wt = ring[:, nth_slab(st, slab, sl) % RING, 0:KC * 32].rearrange("p (k n) -> p k n", k=KC)
                        for k in range(KC):
                            mm = nc.tensor.matmul(ps[0:size, b, 0:width], rhs[:, k, at:at + size],
                                                  wt[:, k, c0:c0 + width], start=(k == 0), stop=(k == KC - 1))
                    else:
                        for k in range(KC):
                            mm = nc.tensor.matmul(bank(b, n), wt[:, k, c0:c0 + P], rhs[:, k, 0:n],
                                                  start=(k == 0), stop=(k == KC - 1))
                    mm.then_inc(s["proj_done"], 1)

            def gdn(q, l):
                qo = view(QO, 12, T1)
                for c in range(8):
                    if c % 4 == 0:
                        await_("act", q, "sq", c // 4)
                    mm = nc.tensor.matmul(ps[:, 4 + c // 2, c % 2 * T1:c % 2 * T1 + T1], ones, sq[:, c, 0:T1],
                                          start=True, stop=True)
                    if c % 2:
                        mark(mm, q, "l2", c // 2)
                await_("dve", q, "k_ready")
                name, value = job_read[proj_end(q) - 1]
                for t in range(2):
                    for what, b in ((4, t), (8, 2 + t)):
                        for i in range(GH):
                            mm = nc.tensor.transpose(ps[:, b, i * P:(i + 1) * P], qo[:, what + i, t * P:(t + 1) * P],
                                                     ident)
                        mark(mm, q, "ktok" if what == 4 else "vtok", t)
                await_("dve", q, "g")
                g8 = view(SMALL + 96, 8)
                await_("act", q, "l2r", 3)
                mark(nc.tensor.matmul(ps[:, 6, 0:8], upper, g8, start=True, stop=True), q, "gc")
                for t in range(2):
                    for i in range(GH):
                        p = GH * t + i
                        mm = nc.tensor.matmul(ps[:, 4 + t, i * P:(i + 1) * P], g8[:, p:p + 1].to_broadcast([P, P]),
                                              upper, start=True, stop=True)
                    mark(mm, q, "gr", t)
                await_("dve", q, "gc")
                for t in range(2):
                    for i in range(GH):
                        kt = qo[:, 4 + i, t * P:(t + 1) * P]
                        mm = nc.tensor.matmul(ps[:, 6 + t, i * P:(i + 1) * P], kt, kt, start=True, stop=True)
                    mark(mm, q, "kk", t)
                tri, uu, pp, lo = view(TT, 8, P), view(UU, 8, P), view(PPP, 8, P), view(LO, 8, P)
                for lev in range(LEVELS):
                    for t in range(2):
                        await_("dve", q, "lo", lev, t)
                        if lev == 0:
                            await_("dve", q, "unit")
                            await_("dve", q, "kbe", t)
                        else:
                            await_("dve", q, "u", lev - 1, t)
                        for i in range(GH):
                            p = GH * t + i
                            mm = nc.tensor.matmul(ps[:, t, i * P:(i + 1) * P], lo[:, p], uu[:, p], start=True, stop=True)
                        mark(mm, q, "p", lev, t)
                    for t in range(2):
                        await_("act", q, "p", lev, t)
                        if lev == 0:
                            await_("dve", q, "vb", t)
                            await_("act", q, "eg", t)
                            await_("dve", q, "gr_read", t)
                        if lev:
                            await_("dve", q, "t", lev - 1, t)
                        for i in range(GH):
                            p = GH * t + i
                            mm = nc.tensor.matmul(ps[:, 2 + t, i * P:(i + 1) * P], tri[:, p], pp[:, p],
                                                  start=True, stop=True)
                        mark(mm, q, "up", lev, t)
                        if lev < LEVELS - 1:
                            for i in range(GH):
                                p = GH * t + i
                                mm = nc.tensor.matmul(ps[:, 4 + t, i * P:(i + 1) * P], pp[:, p], tri[:, p],
                                                      start=True, stop=True)
                            mark(mm, q, "tp", lev, t)
                for t in range(2):
                    await_("dve", q, "l", t)
                    for i in range(GH):
                        mm = nc.tensor.matmul(ps[:, 6 + t, i * P:(i + 1) * P], qo[:, 4 + i, t * P:(t + 1) * P],
                                              qo[:, i, t * P:(t + 1) * P], start=True, stop=True)
                    mark(mm, q, "qk", t)
                kbe, vb, kd = view(KBE, 8, P), view(VB, 8, P), view(KD, 8, P)
                nw, vn, st1, att, qe = view(NW, 4, P), hid_v, view(STATE, 4, P), view(ATT, 8, P), view(QE, 8, P)
                for t in range(2):
                    await_("dve", q, "u", LEVELS - 1, t)
                for i in range(GH):
                    mm = nc.tensor.matmul(ps[:, 1, i * P:(i + 1) * P], kbe[:, GH + i], uu[:, GH + i],
                                          start=True, stop=True)
                mark(mm, q, "w")
                for i in range(GH):
                    mm = nc.tensor.matmul(ps[:, 2, i * P:(i + 1) * P], uu[:, i], vb[:, i], start=True, stop=True)
                mark(mm, q, "vn", 0)
                await_("act", q, "vn", 0)
                for i in range(GH):
                    mm = nc.tensor.matmul(ps[:, 4, i * P:(i + 1) * P], kd[:, i], vn[:, i], start=True, stop=True)
                mark(mm, q, "state")
                await_("dve", q, "att", 0)
                for i in range(GH):
                    mm = nc.tensor.matmul(ps[:, 5, i * P:(i + 1) * P], vn[:, i], att[:, i], start=True, stop=True)
                mark(mm, q, "o", 0)
                await_("act", q, "nw")
                await_("act", q, "state")
                for i in range(GH):
                    nc.tensor.matmul(ps[:, 3, i * P:(i + 1) * P], uu[:, GH + i], vb[:, GH + i], start=True, stop=False)
                    mm = nc.tensor.matmul(ps[:, 3, i * P:(i + 1) * P], nw[:, i], st1[:, i], start=False, stop=True)
                mark(mm, q, "vn", 1)
                await_("act", q, "vn", 1)
                await_("dve", q, "att", 1)
                for i in range(GH):
                    nc.tensor.matmul(ps[:, 6, i * P:(i + 1) * P], vn[:, GH + i], att[:, GH + i], start=True, stop=False)
                    mm = nc.tensor.matmul(ps[:, 6, i * P:(i + 1) * P], st1[:, i], qe[:, GH + i], start=False, stop=True)
                mark(mm, q, "o", 1)
                await_("act", q, "osq")
                for c in range(GH):
                    mm = nc.tensor.matmul(ps[:, c // 2, c % 2 * T1:c % 2 * T1 + T1], ones, sq[:, c, 0:T1],
                                          start=True, stop=True)
                mark(mm, q, "on")

            def nsa_rope(q, l):
                nqk = view(NQK, 7, T1)
                for j in range(7):
                    mm = nc.tensor.matmul(ps[:, 4 + j // 2, j % 2 * T1:j % 2 * T1 + T1], cst("rope"), nqk[:, j],
                                          start=True, stop=True)
                    if j % 2 or j == 6:
                        mark(mm, q, "rot", j // 2)

            def nsa_compressed(q, l):
                hc = view(HC, 2, 2 * NCMP)
                pe.wait_ge(s["proj_act"], act_before(q) + 26)
                await_("dve", q, "roped", 3)
                mark(nc.tensor.matmul(ps[0:64, 4, 0:2 * NCMP], col("w2k", l * 64, 64), hc[:, 0], start=True, stop=True),
                     q, "kcmp")
                for e in range(2):
                    mm = nc.tensor.matmul(ps[0:NCMP, 5, e * 64:e * 64 + 64], hc[:, 1, e * NCMP:(e + 1) * NCMP],
                                          col("w2v", l * 64, 64), start=True, stop=True)
                mark(mm, q, "vcmp")

            def attention(q, st):
                units = attn_units(st)
                pb, pt = view(PB, 2, 2, T2), view(PT, 2, 2, 3 * P)

                def scores(n):
                    br, i, j = units[n]
                    qt, kk, vv, tiles, keys = attn_operands(st, br, i, j)
                    at, qn = tiles[i]
                    if n >= 2:
                        await_("dve", q, "sm", n - 2)
                    for e in range(2):
                        o = ps[0:qn, n % 2 * 2 + e, 0:keys]
                        fox = st[0] == "fox"
                        mm = nc.tensor.matmul(o, qt[64 * e:64 * e + 64, at:at + qn], kk[64 * e:64 * e + 64, 0:keys],
                                              start=True, stop=not fox)
                        if fox:
                            head = 2 * j + e
                            mm = nc.tensor.matmul(o, ident[0:FOXH, head:head + 1].to_broadcast([FOXH, qn]),
                                                  view(NCUM, T2)[0:FOXH, 0:keys], start=False, stop=True)
                    mark(mm, q, "s", n)

                def turn(n):
                    br, i, j = units[n]
                    _, _, vv, tiles, keys = attn_operands(st, br, i, j)
                    qn = tiles[i][1]
                    await_("act", q, "exp", n)
                    if n >= 1:
                        await_("act", q, "pt", n - 1)
                    for e in range(2):
                        for c, (k0, kn, _) in enumerate(vv[e]):
                            mm = nc.tensor.transpose(ps[0:kn, 4 + e, c * P:c * P + qn], pb[0:qn, n % 2, e, k0:k0 + kn],
                                                     ident[0:qn, 0:qn])
                    mark(mm, q, "turn", n)

                def values(n):
                    br, i, j = units[n]
                    _, _, vv, tiles, keys = attn_operands(st, br, i, j)
                    qn = tiles[i][1]
                    await_("act", q, "pt", n)
                    if n >= 2:
                        await_("dve", q, "o", n - 2)
                    for e in range(2):
                        for c, (k0, kn, v) in enumerate(vv[e]):
                            mm = nc.tensor.matmul(ps[0:qn, 6 + n % 2, 64 * e:64 * e + 64],
                                                  pt[0:kn, n % 2, e, c * P:c * P + qn], v,
                                                  start=(c == 0), stop=(c == len(vv[e]) - 1))
                    mark(mm, q, "pv", n)

                scores(0)
                for n in range(len(units) + 1):
                    if n + 1 < len(units):
                        scores(n + 1)
                    if n < len(units):
                        turn(n)
                    if n >= 1:
                        values(n - 1)

            def turn_outputs(q, st):
                tiles = KT1 if st[0] == "mix" else KT2
                chunks = 4 if st[0] == "mix" else KC
                n = 0
                for i, (at, qn) in enumerate(tiles):
                    for j in range(0, chunks, 4):
                        await_("dve", q, *(("o_ready", i) if st[0] == "mix" else ("o", len(attn_units(st)) - 1)))
                        if n >= 4:
                            await_("act", q, "y_att", n - 4)
                        for c in range(4):
                            src = view(OACC, len(tiles), chunks * P)[0:qn, i, (j + c) * P:(j + c + 1) * P]
                            mm = nc.tensor.transpose(ps[:, n % 4, c * P:c * P + qn], src, ident[0:qn, 0:qn])
                        mark(mm, q, "y_att", n)
                        n += 1

            def fox_norms(q, st, slab, job):
                for c in range(2 * KC):
                    await_("act", q, "fsq", c)
                    if c >= 4:
                        await_("act", q, "fln", c - 4)
                    mark(nc.tensor.matmul(bank(4 + c % 4, T2), cst("blk64"), sq[:, c % 8, :], start=True, stop=True),
                         q, "fss", c)
                    if c >= 4:
                        run_jobs(q, st, 12 + c, 13 + c, slab, job)

            def fox_forget(q):
                for t, (at, size) in enumerate(KT2):
                    if t == 0:
                        await_("act", q, "fln", 15)
                    for k in range(KC):
                        mm = nc.tensor.matmul(ps[0:size, 4 + t, 0:FOXH], h[:, k, at:at + size], col("wf", k * FOXH, FOXH),
                                              start=(k == 0), stop=(k == KC - 1))
                    mark(mm, q, "fl", t)
                lf = view(LF, 3, FOXH)
                await_("dve", q, "lf", 2)
                for t, (at, size) in enumerate(KT2):
                    for u in range(t + 1):
                        un = KT2[u][1]
                        m = (upper if u == t else ones)[0:un, 0:size]
                        mm = nc.tensor.matmul(ps[0:size, 4 + t, 0:FOXH], m, lf[0:un, u], start=(u == 0), stop=(u == t))
                    mark(mm, q, "cq", t)
                for t, (at, size) in enumerate(KT2):
                    for u in range(t + 1):
                        un = KT2[u][1]
                        m = (upper if u == t else ones)[0:un, 0:size]
                        mm = nc.tensor.matmul(ps[0:FOXH, 7, at:at + size], lf[0:un, u], m, start=(u == 0), stop=(u == t))
                mark(mm, q, "ck")

            def hg_scan(q):
                e8, sc, kd, kdt, stt = view(HE, 8, P), view(HSC, 8, P), view(HKD, 8, P), view(HKDT, 8, P), view(HST, 8, P)
                qeb, hv = view(HQE, 8, P), view(HV, 3, D)
                hq, hk = view(HQ, KC, T2), view(HK, KC, T2)
                for t, (at, n) in enumerate(KT2):
                    levels = n.bit_length() - 1
                    for lev in range(-1, levels):
                        b = 2 * (lev % 2)
                        if lev >= 0:
                            await_("dve", q, "eq", t, lev)
                        else:
                            await_("dve", q, "hk", KC - 1)
                        if t and lev < 1:
                            await_("dve", q, "hsum", t - 1)
                        if lev >= 1:
                            await_("dve", q, "hmask", t, lev - 2)
                        for i in range(HGH):
                            if lev < 0:
                                lhs, rhs = hk[:, i, at:at + n], hq[:, i, at:at + n]
                            else:
                                lhs = rhs = e8[:, i, 0:n]
                            mm = nc.tensor.matmul(ps[0:n, b + i // 4, i % 4 * P:i % 4 * P + n], lhs, rhs,
                                                  start=True, stop=True)
                        mark(mm, q, "hs", t, lev)
                    if t < 2:
                        await_("dve", q, "hkd", t)
                        if t:
                            await_("dve", q, "hst", t - 1)
                        for i in range(HGH):
                            mm = nc.tensor.transpose(ps[0:n, 4 + i // 4, i % 4 * P:(i % 4 + 1) * P], kd[:, i, 0:n], ident)
                        mark(mm, q, "hkdt", t)
                    await_("dve", q, "hsum", t)
                    await_("act", q, "hqe", t)
                    await_("dve", q, "hqe", t)
                    if t:
                        await_("dve", q, "hst", t - 1)
                        await_("act", q, "ho", t - 1)
                    for i in range(HGH):
                        o = ps[:, 6 + i // 4, i % 4 * P:i % 4 * P + n]
                        mm = nc.tensor.matmul(o, hv[0:n, t, i * P:(i + 1) * P], sc[0:n, i, 0:n], start=True,
                                              stop=(t == 0))
                        if t:
                            mm = nc.tensor.matmul(o, stt[:, i], qeb[:, i, 0:n], start=False, stop=True)
                    mark(mm, q, "ho", t)
                    if t < 2:
                        await_("act", q, "hkdt", t)
                        for i in range(HGH):
                            mm = nc.tensor.matmul(ps[:, 4 + i // 4, i % 4 * P:(i % 4 + 1) * P], kdt[0:n, i],
                                                  hv[0:n, t, i * P:(i + 1) * P], start=True, stop=True)
                        mark(mm, q, "hst", t)
                for c in range(HGH):
                    await_("act", q, "hosq", c // 4)
                    if c >= 4:
                        await_("act", q, "hon0", c - 4)
                    mark(nc.tensor.matmul(bank(c % 4, T2), ones, sq[:, c, :], start=True, stop=True), q, "hon", c)

            def sort_tokens(q, l):
                m3 = view(MM, 3, NE)
                for t, (at, size) in enumerate(KT2):
                    await_("dve", q, "m", t)
                for t, (at, size) in enumerate(KT2):
                    for u in range(t + 1):
                        un = KT2[u][1]
                        tri = (upper if u == t else ones)[0:un, 0:size]
                        mm = nc.tensor.matmul(ps[0:size, 4 + t, 0:NE], tri, m3[0:un, u], start=(u == 0), stop=(u == t))
                    mark(mm, q, "rank", t)
                await_("act", q, "gtt")
                for u in range(3):
                    un = KT2[u][1]
                    mm = nc.tensor.matmul(ps[:, 7, 0:NE], ones[0:un], m3[0:un, u], start=(u == 0), stop=(u == 2))
                mark(mm, q, "count")
                n = 0
                for t, (at, size) in enumerate(KT2):
                    for b in range(2):
                        if n >= 4:
                            await_("act", q, "htok", n - 4)
                        for i in range(4):
                            mm = nc.tensor.transpose(ps[0:size, n % 4, i * P:(i + 1) * P], h[:, 4 * b + i, at:at + size],
                                                     ident)
                        mark(mm, q, "htok", n)
                        n += 1
                htok, pm, pw = view(HTOK, 3, D), view(PM, 3, SLOTS), view(PW, 3, SLOTS)
                for i in range(6):
                    await_("act", q, "htok", i)
                for t in range(3):
                    await_("dve", q, "pm", t)
                for k in range(KC):
                    for b in range(2):
                        n = 2 * k + b
                        if n >= 4:
                            await_("act", q, "xs", n - 4)
                        for t, (at, size) in enumerate(KT2):
                            mm = nc.tensor.matmul(bank(n % 4, T2), htok[0:size, t, k * P:(k + 1) * P],
                                                  pm[0:size, t, b * T2:(b + 1) * T2], start=(t == 0), stop=(t == 2))
                        mark(mm, q, "xs", n)
                for t in range(3):
                    await_("dve", q, "pw", t)
                for c in range(5):
                    cn = min(P, SLOTS - c * P)
                    if c < 3:
                        await_("dve", q, "pos", 2)
                    else:
                        await_("dve", q, "gp", c - 3)
                    for t, (at, size) in enumerate(KT2):
                        mm = nc.tensor.transpose(ps[0:cn, 4 + c % 3, at:at + size], pw[0:size, t, c * P:c * P + cn],
                                                 ident[0:size, 0:size])
                    mark(mm, q, "gp", c)

            def sparse_pe(q, l, slab, t0):
                mark2, await2 = stepper("pe", l)
                steps = 2 * NE

                def up_s(k):
                    t = t0 + k
                    if k % 2 == 0:
                        w(f"xe_ready{l}", k // 2 + 1, 4)
                    if k >= 2:
                        w("hid_done", 2 * (t - 1), 16)
                    i = slab + (0 if k == 0 else 2 + 3 * (k - 1))
                    for j, b in ((0, 0), (1, 2)):
                        slab_in(i + j)
                        wt = slab_view(i + j)
                        for f in range(2):
                            for c in range(KC):
                                mm = nc.tensor.matmul(ps[:, b + k % 2, f * W:(f + 1) * W], wt[:, c, f * P:(f + 1) * P],
                                                      view(XE, 2, KC, W)[:, k // 2 % 2, c], start=(c == 0),
                                                      stop=(c == KC - 1))
                    mm.then_inc(s["up_done"], 2)

                def down_s(k):
                    t = t0 + k
                    i = slab + (4 if k + 1 < steps else 2) + 3 * k
                    wt = slab_view(i, 2)
                    w("hid_done", 2 * t + 2, 16)
                    slab_in(i)
                    if k % 2 == 0 and k >= 4:
                        w("y_added", KC * (t - 2), 8 * KC)
                    for f in range(2):
                        for d in range(KC):
                            mm = nc.tensor.matmul(ps[:, 4 + k // 2 % 2, d * W:(d + 1) * W], wt[:, f, d * P:(d + 1) * P],
                                                  hid[:, k % 2, f, 0:W], start=(k % 2 == 0 and f == 0 and d == 0),
                                                  stop=(k % 2 == 1 and f == 1), skip_group_check=True)
                    mm.then_inc(s["y_done"], KC)

                def step(k):
                    if k + 1 < steps:
                        up_s(k + 1)
                    down_s(k)

                up_s(0)
                for k in range(8):
                    step(k)
                with pe.Fori(0, steps // 8 - 2) as it:
                    trip[0] = it
                    for k in range(8, 16):
                        step(k)
                    trip[0] = None
                for k in range(steps - 8, steps):
                    step(k)
                ys, yt, gp = view(YS, KC, SLOTS + W), view(YT, 5, D), view(GP, 5, T2)
                await2("dve", "ys")
                n = 0
                for c in range(5):
                    cn = min(P, SLOTS - c * P)
                    for b in range(2):
                        if n >= 4:
                            await2("act", "yt", n - 4)
                        for i in range(4):
                            mm = nc.tensor.transpose(ps[0:cn, n % 4, i * P:(i + 1) * P],
                                                     ys[:, 4 * b + i, c * P:c * P + cn], ident)
                        mark2(mm, "yt", n)
                        n += 1
                for i in range(10):
                    await2("act", "yt", i)
                for d in range(KC):
                    if d >= 4:
                        pe.wait_ge(s["y_added"], KC * (t0 + steps) - 2 * KC + 2 * (d - 3))
                    for c in range(5):
                        cn = min(P, SLOTS - c * P)
                        mm = nc.tensor.matmul(bank(d % 4, T2), yt[0:cn, c, d * P:(d + 1) * P], gp[0:cn, c],
                                              start=(c == 0), stop=(c == 4))
                    mark2(mm, "y", d)

            def route(q, l):
                wr = col("wr", l * KC * 36, KC * 36).rearrange("p (k n) -> p k n", k=KC)
                for t, (at, size) in enumerate(KT2):
                    for k in range(KC):
                        mm = nc.tensor.matmul(ps[0:size, 4 + t, 0:36], h[:, k, at:at + size],
                                              wr[:, k], start=(k == 0), stop=(k == KC - 1))
                    mark(mm, q, "logits", t)
                for t, (at, size) in enumerate(KT2):
                    await_("dve", q, "gates", t)
                    mm = nc.tensor.transpose(ps[0:NE, 7, at:at + size], view(GT, 3, NE)[0:size, t], ident[0:size, 0:size])
                mark(mm, q, "gt")

            def dense_pe(q, l, slab, t0):
                steps = 2 * NE

                def spread_gates(e):
                    w(f"gb_in{l}", e + 1, 4)
                    if e:
                        w(f"gb_ready{l}", e, 4)
                    nc.tensor.matmul(bank(6, T2), ones[0:NE], view(GSEL, 2, T2)[0:NE, e % 2], start=True, stop=True)\
                        .then_inc(s[f"gb_ps{l}"], 1)

                def step(k):
                    if k + 1 < steps:
                        if (k + 1) % 2 == 0:
                            spread_gates((k + 1) // 2)
                        up(t0 + k + 1, slab + 2 + 3 * k, T2)
                    down(t0 + k, k % 2, slab + (4 if k + 1 < steps else 2) + 3 * k, T2, first=(t0 + k == 0))

                await_("act", q, "xs", 2 * KC - 1)
                await_("dve", q, "gp", 4)
                spread_gates(0)
                up(t0, slab, T2, first=(t0 == 0))
                for k in range(8):
                    step(k)
                with pe.Fori(0, steps // 8 - 2) as it:
                    trip[0] = it
                    for k in range(8, 16):
                        step(k)
                    trip[0] = None
                for k in range(steps - 8, steps):
                    step(k)

            def moe_pe(q, l, slab, t0):
                route(q, l)
                sort_tokens(q, l)
                await_("dve", q, "ints")
                most = pe.value_load(most_at, min_val=0, max_val=T2)
                with pe.If(most > W):
                    dense_pe(q, l, slab, t0)
                with pe.Else():
                    sparse_pe(q, l, slab, t0)

            def norm(n_norm, n):
                for k in range(KC):
                    if k % 4 == 0:
                        pe.wait_ge(s["sq_ready"], 2 * n_norm + k // 4 + 1)
                    mm = nc.tensor.matmul(bank(7, n), ones, sq[:, k, 0:n], start=(k == 0), stop=(k == KC - 1))
                mm.then_inc(s["ss_ready"], 1)

            def ada_cols(n, j):
                pe.wait_ge(s["ada_acc"], n + 1)
                for f in range(2):
                    mm = nc.tensor.matmul(ps[:, 6, 300 + 2 * j + f:301 + 2 * j + f], acc[:, n % 4, f * P:(f + 1) * P],
                                          ones[:, 0:1], start=True, stop=True)
                mm.then_inc(s["ada_ps"], 1)

            def share_cols(st, step, n, m):
                _, lo, hi = ada_share(st[1], st[2], step)
                if hi > lo:
                    pe.wait_ge(s["ada_col"], m)
                    for j in range(hi - lo):
                        ada_cols(n + j, j)
                return n + hi - lo, m + (hi > lo)

            def thirds(out, w_hi, w_lo, v_hi, v_lo, start, stop):
                nc.tensor.matmul(out, w_hi, v_hi, start=start, stop=False)
                nc.tensor.matmul(out, w_hi, v_lo, start=False, stop=False)
                return nc.tensor.matmul(out, w_lo, v_hi, start=False, stop=stop)

            def up_split(t, i, n, first=False):
                for f in range(2):
                    u = 2 * t + f
                    if not (first and f < 2):
                        pe.wait_ge(s["hid_done"], u - 1)
                    for j, b in ((0, 0), (1, 2)):
                        if f == 0:
                            pe.wait_ge(s["w_lo"], split_at[i + j] + 1)
                        hi, lo = hi_slab(i + j), low_view(i + j)
                        cols = slice(f * P, (f + 1) * P)
                        for k in range(KC):
                            mm = thirds(bank(b + f, n), hi[:, k, cols], lo[:, k, cols], hh_hi[:, k], hh_lo[:, k],
                                        k == 0, k == KC - 1)
                    mm.then_inc(s["up_done"], 1)

            def down_split(t, i, n, first=False):
                hi, lo = hi_slab(i, 2), low_view(i, 2)
                pe.wait_ge(s["hid_done"], 2 * t + 2)
                pe.wait_ge(s["w_lo"], split_at[i] + 1)
                for d in range(KC):
                    if not (first and d < 2):
                        pe.wait_ge(s["y_added"], KC * t + d - 1)
                    cols = slice(d * P, (d + 1) * P)
                    for f in range(2):
                        mm = thirds(bank(4 + d % 2, n), hi[:, f, cols], lo[:, f, cols], hid_hi[:, t % 2, f],
                                    hid_lo[:, t % 2, f], f == 0, f == 1)
                    mm.then_inc(s["y_done"], 1)

            def up(t, i, n, first=False):
                for f in range(2):
                    u = 2 * t + f
                    if not (first and f < 2):
                        w("hid_done", u - 1, 16)
                    for j, b in ((0, 0), (1, 2)):
                        if f == 0:
                            slab_in(i + j)
                        wt = slab_view(i + j)
                        for k in range(KC):
                            mm = nc.tensor.matmul(bank(b + f, n), wt[:, k, f * P:(f + 1) * P], h[:, k, 0:n],
                                                  start=(k == 0), stop=(k == KC - 1))
                    mm.then_inc(s["up_done"], 1)

            def down(t, par, i, n, first=False):
                wt = slab_view(i, 2)
                w("hid_done", 2 * t + 2, 16)
                slab_in(i)
                for d in range(KC):
                    if not (first and d < 2):
                        w("y_added", KC * t + d - 1, 8 * KC)
                    for f in range(2):
                        mm = nc.tensor.matmul(bank(4 + d % 2, n), wt[:, f, d * P:(d + 1) * P], hid[:, par, f, 0:n],
                                              start=(f == 0), stop=(f == 1))
                    mm.then_inc(s["y_done"], 1)

            pe.wait_ge(s["consts"], 32)
            slab = t = n_norm = n_ada = n_share = n_mul = n_ready = n_ffn = 0
            for q, st in enumerate(stages):
                slab = slab_at[q]
                if st[0] == "ada":
                    for a in range(st[2], st[3]):
                        ada_cols(n_ada, a - st[2])
                        n_ada += 1
                    n_share += 1
                    continue
                n, _, shift = norm_of(st)
                norm(n_norm, n)
                n_norm += 1
                n_mul += KC
                n_ready += KC if shift else 0
                if st[0] == "final":
                    continue
                pe.wait_ge(s["h_ready" if shift else "h_mul"], n_ready if shift else n_mul)
                if st[0] == "ffn":
                    pe.wait_ge(s["h_lo"], KC * (n_ffn + 1))
                    n_ffn += 1
                    up_split(t, slab, n, first=(t == 0))
                    slab += 2
                    for a in range(FFN_STEPS):
                        if a + 1 < FFN_STEPS:
                            up_split(t + 1, slab, n)
                            slab += 2
                        if a:
                            n_ada, n_share = share_cols(st, a - 1, n_ada, n_share)
                        down_split(t, slab, n, first=(t == 0))
                        t += 1
                        _, lo, hi = ada_share(st[1], st[2], a)
                        slab += 1 + hi - lo
                    n_ada, n_share = share_cols(st, FFN_STEPS - 1, n_ada, n_share)
                elif st[0] == "mix":
                    job = job_at[q]
                    run_jobs(q, st, 0, 30, slab, job)
                    pe.wait_ge(s["proj_act"], act_before(q) + 24)
                    pe.wait_ge(s["proj_dve"], dve_before(q) + 6)
                    ada_cols(n_ada + ADA_PART - 1, ADA_PART - 1)
                    n_ada += ADA_PART
                    n_share += 1
                    pe.wait_ge(s["ada_col"], n_share)
                    nsa_rope(q, st[1])
                    await_("dve", q, "roped", 3)
                    gdn(q, st[1])
                    await_("dve", q, "y_gdn")
                    await_("act", q, "kc2")
                    run_jobs(q, st, 30, 32, slab, job)
                    nsa_compressed(q, st[1])
                    await_("act", q, "cmp")
                    attention(q, st)
                    turn_outputs(q, st)
                    await_("act", q, "y_att", 1)
                    run_jobs(q, st, 32, 40, slab, job)
                    slab += 20
                elif st[0] == "fox":
                    job = job_at[q]
                    run_jobs(q, st, 0, 16, slab, job)
                    fox_norms(q, st, slab, job)
                    fox_forget(q)
                    pe.wait_ge(s["proj_act"], act_before(q) + 12)
                    await_("dve", q, "fqs")
                    await_("dve", q, "cqc", 2)
                    await_("act", q, "ncum")
                    attention(q, st)
                    turn_outputs(q, st)
                    await_("act", q, "y_att", 5)
                    run_jobs(q, st, 28, 36, slab, job)
                    slab += 16
                elif st[0] == "hg":
                    job = job_at[q]
                    run_jobs(q, st, 0, 36, slab, job)
                    pe.wait_ge(s["proj_act"], act_before(q) + 36)
                    hg_scan(q)
                    await_("dve", q, "y_hg")
                    run_jobs(q, st, 36, 44, slab, job)
                    slab += 20
                elif st[0] == "moe":
                    moe_pe(q, st[1], slab, t)
                    slab += 6 * NE
                    t += 2 * NE
        @block.scalar
        def _(act):
            chain = [0]
            trip = [None]

            def w(name, value, per_trip):
                act.wait_ge(s[name], value if trip[0] is None else trip[0] * per_trip + value)

            def link(ins):
                chain[0] += 1
                ins.then_inc(s["act_chain"], 1)
                act.wait_ge(s["act_chain"], chain[0])

            def split_hi(i):
                m = split_at[i]
                slab_here(act, i)
                if m >= HI_RING:
                    name, value = free[split_slabs[m - HI_RING]]
                    act.wait_ge(s[name], value)
                nc.scalar.copy(hi_slab(i), slab_view(i)).then_inc(s["w_hi"], 1)

            mark, await_ = stepper("act")

            def take(j):
                act.wait_ge(s["proj_done"], j + 1)

            def gdn(q, l):
                qi, qo = view(QI, 12, T1 + 3), view(QO, 12, T1)
                for g in range(3):
                    await_("dve", q, "conv", g)
                    ins = nc.scalar.activation(qo[:, 4 * g:4 * g + 4], qo[:, 4 * g:4 * g + 4], ACT.Silu)
                    mark(ins, q, "qkv", g)
                for g in range(2):
                    await_("act", q, "qkv", g)
                    mark(nc.scalar.activation(sq[:, 4 * g:4 * g + 4, 0:T1], qo[:, 4 * g:4 * g + 4], ACT.Square), q, "sq", g)
                nc.scalar.preload_act_table_set("natural_log_exp_and_others")
                for b in range(4):
                    await_("pe", q, "l2", b)
                    r = sq[:, 2 * b:2 * b + 2, 0:T1]
                    mark(nc.scalar.activation(r, ps[:, 4 + b, :].rearrange("p (a n) -> p a n", a=2), ACT.Ln, bias=eps),
                         q, "l2r", b)
                for b in range(4):
                    await_("act", q, "l2r", b)
                    r = sq[:, 2 * b:2 * b + 2, 0:T1]
                    mark(nc.scalar.activation(r, r, ACT.Exp, scale=-0.5), q, "rn", b)
                ba, sg, u8, sp, ea, na = (view(SMALL, 2, 32), view(SMALL + 128, 2, 28), view(SMALL + 184, 2, 4),
                                          view(SMALL + 192, 2, 4), view(SMALL + 200, 4), view(SMALL + 204, 2, 4))
                dve_read = job_read[proj_end(q) - 1]
                act.wait_ge(s[dve_read[0]], dve_read[1])
                mark(nc.scalar.activation(sg, ba[:, :, 0:28], ACT.Exp, scale=-1.0), q, "sg")
                mark(nc.scalar.activation(ea, col("a_log", l * GH, GH), ACT.Exp), q, "ea")
                await_("dve", q, "na")
                mark(nc.scalar.activation(na, na, ACT.Exp), q, "na0")
                await_("act", q, "na0")
                mark(nc.scalar.activation(na, na, ACT.Ln, bias=1.0), q, "na")
                dect, dd, egr = view(DECT, 8, P), view(LL, 8, P), view(QE, 8, P)
                for t in range(2):
                    await_("dve", q, "gr_read", t)
                    mark(nc.scalar.activation(egr[:, 4 * t:4 * t + 4], ps[:, 4 + t, :].rearrange("p (a n) -> p a n", a=4),
                                              ACT.Exp), q, "eg", t)
                mark(nc.scalar.activation(view(SMALL + 232, 8), view(SMALL + 216, 8), ACT.Exp), q, "egc")
                mark(nc.scalar.activation(view(SMALL + 240, 8), view(SMALL + 224, 8), ACT.Exp), q, "ed")
                for t in range(2):
                    mark(nc.scalar.activation(dect[:, 4 * t:4 * t + 4], dect[:, 4 * t:4 * t + 4], ACT.Exp), q, "dect", t)
                    mark(nc.scalar.activation(dd[:, 4 * t:4 * t + 4], dd[:, 4 * t:4 * t + 4], ACT.Exp, scale=-1.0),
                         q, "dd", t)
                pp = view(PPP, 8, P)
                for lev in range(LEVELS):
                    for t in range(2):
                        await_("pe", q, "p", lev, t)
                        if lev:
                            await_("pe", q, "tp", lev - 1, t)
                        mark(nc.scalar.copy(pp[:, 4 * t:4 * t + 4], ps[:, t, :].rearrange("p (a n) -> p a n", a=4)),
                             q, "p", lev, t)
                four = lambda b: ps[:, b, :].rearrange("p (a n) -> p a n", a=4)
                nw, vn, st1, ot = view(NW, 4, P), hid_v, view(STATE, 4, P), view(OT, 4, T1)
                await_("pe", q, "w")
                mark(nc.scalar.activation(nw, four(1), ACT.Copy, scale=-1.0), q, "nw")
                await_("pe", q, "vn", 0)
                mark(nc.scalar.copy(vn[:, 0:4], four(2)), q, "vn", 0)
                await_("pe", q, "state")
                mark(nc.scalar.copy(st1, four(4)), q, "state")
                await_("pe", q, "o", 0)
                mark(nc.scalar.copy(ot[:, :, 0:P], four(5)), q, "ot", 0)
                await_("pe", q, "vn", 1)
                mark(nc.scalar.copy(vn[:, 4:8], four(3)), q, "vn", 1)
                await_("pe", q, "o", 1)
                mark(nc.scalar.copy(ot[:, :, P:T1], four(6)), q, "ot", 1)
                await_("act", q, "ot", 1)
                mark(nc.scalar.activation(sq[:, 0:4, 0:T1], ot, ACT.Square), q, "osq")
                await_("pe", q, "on")
                for b in range(2):
                    mark(nc.scalar.activation(sq[:, 2 * b:2 * b + 2, 0:T1], ps[:, b, :].rearrange("p (a n) -> p a n", a=2),
                                              ACT.Ln, scale=1.0 / P, bias=eps), q, "on0", b)
                await_("act", q, "on0", 1)
                mark(nc.scalar.activation(sq[:, 0:4, 0:T1], sq[:, 0:4, 0:T1], ACT.Exp, scale=-0.5), q, "on")

            def nsa_blocks(q, l, job):
                kc2, nqk = view(KC2, 2, 2, T1), view(NQK, 7, T1)
                await_("dve", q, "roped", 2)
                act.wait_ge(s["proj_act"], act_before(q) + 22)
                for c, src in enumerate((nqk[:, 4], view(VC, T1))):
                    for g in range(2):
                        nc.scalar.copy(kc2[0:64, c, g, :], src[64 * g:64 * g + 64, :])
                        ins = nc.scalar.copy(kc2[64:128, c, g, 0:T1 - 1], src[64 * g:64 * g + 64, 1:T1])
                mark(ins, q, "kc2")

            def attention(q, st):
                units = attn_units(st)
                pb, pt = view(PB, 2, 2, T2), view(PT, 2, 2, 3 * P)
                stat = view(STAT, 2, 3, 2)
                scale = 0.125 if st[0] == "mix" else 1.0

                def exp(n):
                    br, i, j = units[n]
                    tiles, keys = attn_operands(st, br, i, j)[3:]
                    qn = tiles[i][1]
                    await_("dve", q, "nm", n)
                    for e in range(2):
                        ins = nc.scalar.activation(pb[0:qn, n % 2, e, 0:keys], pb[0:qn, n % 2, e, 0:keys], ACT.Exp,
                                                   bias=stat[0:qn, n % 2, 1, e:e + 1], scale=scale,
                                                   accum_out=stat[0:qn, n % 2, 2, e:e + 1])
                    mark(ins, q, "exp", n)

                def copy(n):
                    br, i, j = units[n]
                    _, _, vv, tiles, keys = attn_operands(st, br, i, j)
                    qn = tiles[i][1]
                    await_("pe", q, "turn", n)
                    if n >= 2:
                        await_("pe", q, "pv", n - 2)
                    for e in range(2):
                        c = 0
                        if vv[e][0][1] < P:
                            kn = vv[e][0][1]
                            ins = nc.scalar.copy(pt[0:kn, n % 2, e, 0:qn], ps[0:kn, 4 + e, 0:qn])
                            c = 1
                        if c < len(vv[e]):
                            m = len(vv[e])
                            ins = nc.scalar.copy(pt[:, n % 2, e, c * P:m * P], ps[:, 4 + e, c * P:m * P])
                    mark(ins, q, "pt", n)

                for n in range(len(units)):
                    exp(n)
                    copy(n)

            def nsa_root(q):
                r8 = view(STAT + 32, 8)
                for i in range(2):
                    await_("dve", q, "oss", i)
                    nc.scalar.preload_act_table_set("natural_log_exp_and_others")
                    mark(nc.scalar.activation(r8, r8, ACT.Ln, scale=1.0 / 64, bias=eps), q, "orms0", i)
                    await_("act", q, "orms0", i)
                    mark(nc.scalar.activation(r8, r8, ACT.Exp, scale=-0.5), q, "orms", i)

            def take_outputs(q, st):
                tiles = KT1 if st[0] == "mix" else KT2
                chunks, gain = (4, col("nsa_g", st[1])) if st[0] == "mix" else (KC, 1.0)
                n = 0
                for i, (at, qn) in enumerate(tiles):
                    for j in range(0, chunks, 4):
                        await_("pe", q, "y_att", n)
                        first = (4 if st[0] == "mix" else 0) + j
                        src = ps[:, n % 4, :].rearrange("p (a n) -> p a n", a=4)[:, :, 0:qn]
                        mark(nc.scalar.activation(h[:, first:first + 4, at:at + qn], src, ACT.Copy, scale=gain),
                             q, "y_att", n)
                        n += 1

            def fox_act(q, job):
                def square(c):
                    act.wait_ge(s["proj_dve"], dve_before(q) + c + 1)
                    mark(nc.scalar.activation(sq[:, c % 8, :], fox_chunk(c), ACT.Square), q, "fsq", c)

                for c in range(KC):
                    square(c)
                nc.scalar.preload_act_table_set("natural_log_exp_and_others")
                for c in range(2 * KC):
                    root(q, c)
                    if c < KC:
                        await_("dve", q, "fn", c)
                        square(c + KC)
                    if c >= 4:
                        value_in(q, job, 12 + c)

            def root(q, c):
                await_("pe", q, "fss", c)
                mark(nc.scalar.activation(sq[:, c % 8, :], bank(4 + c % 4, T2), ACT.Ln, scale=1.0 / FOXD, bias=eps),
                     q, "fln", c)
                await_("act", q, "fln", c)
                mark(nc.scalar.activation(sq[:, c % 8, :], sq[:, c % 8, :], ACT.Exp, scale=-0.5), q, "frn", c)

            def value_in(q, job, i):
                idx = stage_jobs(("fox",))[i][1]
                act.wait_ge(s["proj_done"], job + i + 1)
                size = KT2[idx[1]][1]
                nc.scalar.copy(view(FV, 3, D)[0:size, idx[1], idx[0] * COLS:(idx[0] + 1) * COLS],
                               ps[0:size, (job + i) % 4, 0:COLS]).then_inc(s["proj_act"], 1)

            def fox_forget(q):
                a, b = view(LF + 48, 3, FOXH), view(LF + 96, 3, FOXH)
                for t, (at, size) in enumerate(KT2):
                    await_("dve", q, "fabs", t)
                    mark(nc.scalar.activation(b[0:size, t], b[0:size, t], ACT.Exp), q, "fe", t)
                for t, (at, size) in enumerate(KT2):
                    await_("act", q, "fe", t)
                    mark(nc.scalar.activation(b[0:size, t], b[0:size, t], ACT.Ln, bias=1.0), q, "fl", t)
                await_("pe", q, "ck")
                mark(nc.scalar.activation(view(NCUM, T2)[0:FOXH], ps[0:FOXH, 7, 0:T2], ACT.Copy, scale=-1.0), q, "ncum")

            def hg_act(q, job, st):
                hq, hk, hb, hgt = view(HQ, KC, T2), view(HK, KC, T2), view(HB, KC, T2), view(HG, KC, T2)
                lbs = view(HLB, 4, KC)
                await_("dve", q, "lb0")
                mark(nc.scalar.activation(lbs[:, 0:2], lbs[:, 0:2], ACT.Exp), q, "lb")
                order = [i for i, j in enumerate(stage_jobs(st)) if j[4] == "act"]
                for i in order:
                    kind, idx, _, _, _ = stage_jobs(st)[i]
                    if kind == "hgate" and idx == 0:
                        nc.scalar.preload_act_table_set("natural_log_exp_and_others")
                        for c in range(KC):
                            await_("dve", q, "hk", c)
                            mark(nc.scalar.activation(hb[:, c], hb[:, c], ACT.Ln), q, "lf", c)
                    act.wait_ge(s["proj_done"], job + i + 1)
                    src = bank((job + i) % 4, T2)
                    if kind == "hq" and idx < KC:
                        ins = nc.scalar.activation(hq[:, idx], src, ACT.Silu)
                    elif kind == "hq":
                        ins = nc.scalar.activation(hk[:, idx - KC], src, ACT.Sigmoid, bias=col("hg_bf", idx - KC))
                    elif kind == "hv":
                        size = KT2[idx[1]][1]
                        ins = nc.scalar.copy(view(HV, 3, D)[0:size, idx[1], idx[0] * COLS:(idx[0] + 1) * COLS],
                                             ps[0:size, (job + i) % 4, 0:COLS])
                    else:
                        ins = nc.scalar.activation(hgt[:, idx], src, ACT.Silu)
                    ins.then_inc(s["proj_act"], 1)
                nc.scalar.preload_act_table_set("natural_log_exp_and_others")
                e8, kd, qeb, kdt, ho = view(HE, 8, P), view(HKD, 8, P), view(HQE, 8, P), view(HKDT, 8, P), view(HO, KC, T2)
                for t, (at, n) in enumerate(KT2):
                    await_("dve", q, "cum", t)
                    if t:
                        await_("pe", q, "ho", t - 1)
                    mark(nc.scalar.activation(qeb[:, :, 0:n], hb[:, :, at:at + n], ACT.Exp), q, "hqe", t)
                    await_("dve", q, "kdd", t)
                    mark(nc.scalar.activation(kd[:, :, 0:n], kd[:, :, 0:n], ACT.Exp), q, "kdd", t)
                    if t == 1:
                        mark(nc.scalar.activation(view(HEB, 8), hb[:, :, at + n - 1], ACT.Exp), q, "heb")
                    for lev in range(n.bit_length() - 1):
                        await_("dve", q, "dif", t, lev)
                        sz = 1 << lev
                        v = e8[:, :, 0:n].rearrange("p h (m a b) -> p h m a b", a=2, b=sz)
                        nc.scalar.activation(v[:, :, :, 0], v[:, :, :, 0], ACT.Exp, scale=-1.0)
                        mark(nc.scalar.activation(v[:, :, :, 1], v[:, :, :, 1], ACT.Exp), q, "ee", t, lev)
                    if t < 2:
                        await_("pe", q, "hkdt", t)
                        if t:
                            await_("pe", q, "hst", t - 1)
                        for b in range(2):
                            ins = nc.scalar.copy(kdt[0:n, 4 * b:4 * b + 4],
                                                 ps[0:n, 4 + b, :].rearrange("p (a n) -> p a n", a=4))
                        mark(ins, q, "hkdt", t)
                    await_("pe", q, "ho", t)
                    for b in range(2):
                        ins = nc.scalar.copy(ho[:, 4 * b:4 * b + 4, at:at + n],
                                             ps[:, 6 + b, :].rearrange("p (a n) -> p a n", a=4)[:, :, 0:n])
                    mark(ins, q, "ho", t)
                await_("act", q, "ho", 2)
                for b in range(2):
                    mark(nc.scalar.activation(sq[:, 4 * b:4 * b + 4], ho[:, 4 * b:4 * b + 4], ACT.Square), q, "hosq", b)
                for c in range(KC):
                    await_("pe", q, "hon", c)
                    mark(nc.scalar.activation(sq[:, c], bank(c % 4, T2), ACT.Ln, scale=1.0 / P, bias=eps), q, "hon0", c)
                await_("act", q, "hon0", KC - 1)
                mark(nc.scalar.activation(sq[:], sq[:], ACT.Exp, scale=-0.5), q, "hon")

            def sort_tokens(q, l):
                htok, xs = view(HTOK, 3, D), view(XS, KC, SLOTS + W)
                n = 0
                for t, (at, size) in enumerate(KT2):
                    for b in range(2):
                        await_("pe", q, "htok", n)
                        mark(nc.scalar.copy(htok[0:size, t, 4 * b * P:4 * (b + 1) * P], ps[0:size, n % 4, :]), q, "htok", n)
                        n += 1
                for k in range(KC):
                    for b in range(2):
                        n = 2 * k + b
                        await_("pe", q, "xs", n)
                        if n == 0:
                            await_("dve", q, "xpad")
                        mark(nc.scalar.copy(xs[:, k, b * T2:(b + 1) * T2], bank(n % 4, T2)), q, "xs", n)

            def sparse_act(q, l, t0):
                mark2, await2 = stepper("act", l)
                steps = 2 * NE

                def gather(e):
                    at = act.value_load(expert_at(e, trip[0]), min_val=0, max_val=SLOTS)
                    if e >= 2:
                        w("up_done", 2 * t0 + 4 * (e - 1), 16)
                    nc.scalar.copy(view(XE, 2, KC, W)[:, e % 2], view(XS, KC, SLOTS + W)[:, :, bass.ds(at, W)])\
                        .then_inc(s[f"xe_ready{l}"], 1)

                def step(k):
                    if k % 2 == 0 and k // 2 + 1 < NE:
                        gather(k // 2 + 1)
                    t = t0 + k
                    w("up_done", 2 * t + 2, 16)
                    if k >= 2:
                        w("hid_done", 2 * (t - 1), 16)
                    nc.scalar.activation(sil[:, k % 2, 0:2 * W], ps[:, k % 2, 0:2 * W], ACT.Silu)\
                        .then_inc(s["silu_done"], 2)

                await_("act", q, "xs", 2 * KC - 1)
                gather(0)
                for k in range(8):
                    step(k)
                with act.Fori(0, steps // 8 - 2) as it:
                    trip[0] = it
                    for k in range(8, 16):
                        step(k)
                    trip[0] = None
                for k in range(steps - 8, steps):
                    step(k)
                yt = view(YT, 5, D)
                for n in range(10):
                    c, b = n // 2, n % 2
                    cn = min(P, SLOTS - c * P)
                    await2("pe", "yt", n)
                    mark2(nc.scalar.copy(yt[0:cn, c, 4 * b * P:4 * (b + 1) * P], ps[0:cn, n % 4, :]), "yt", n)

            def route(q, l):
                for t in (0, 1, 2):
                    size = KT2[t][1]
                    r = view(RT + 160 * t, 160)[0:size]
                    await_("dve", q, "top", t)
                    nc.scalar.activation(r[:, 64:68], r[:, 36:40], ACT.Exp, bias=r[:, 60:61], accum_out=r[:, 61:62])
                    mark(nc.scalar.activation(r[:, 62:63], r[:, 89:90], ACT.Exp, bias=r[:, 63:64]), q, "pair", t)
                await_("pe", q, "gt")
                mark(nc.scalar.copy(view(GTT, T2)[0:NE], ps[0:NE, 7, 0:T2]), q, "gtt")

            def dense_act(q, l, t0):
                steps = 2 * NE

                def gates(e):
                    w(f"gb_ps{l}", e + 1, 4)
                    nc.scalar.copy(view(GBC, 2, T2)[:, e % 2], bank(6, T2)).then_inc(s[f"gb_ready{l}"], 1)

                def step(k):
                    if k % 2 == 0:
                        if k >= 4:
                            w("hid_done", 2 * (t0 + k - 2), 16)
                        gates(k // 2)
                    for f in range(2):
                        u = 2 * (t0 + k) + f
                        if u >= 2:
                            w("hid_done", u - 1, 16)
                        silu(u, f, T2)

                for k in range(8):
                    step(k)
                with act.Fori(0, steps // 8 - 2) as it:
                    trip[0] = it
                    for k in range(8, 16):
                        step(k)
                    trip[0] = None
                for k in range(steps - 8, steps):
                    step(k)

            def moe_act(q, l, t0):
                route(q, l)
                sort_tokens(q, l)
                await_("dve", q, "ints")
                most = act.value_load(most_at, min_val=0, max_val=T2)
                with act.If(most > W):
                    dense_act(q, l, t0)
                with act.Else():
                    sparse_act(q, l, t0)

            def norm(q, n_norm, n_h, n, shift, splits=()):
                name, value = written[q]
                act.wait_ge(s[name], value)
                for i in range(2):
                    nc.scalar.activation(sq[:, 4 * i:4 * i + 4, 0:n], x[:, 4 * i:4 * i + 4, T2 - n:T2], ACT.Square)\
                        .then_inc(s["sq_ready"], 1)
                for i in splits:
                    split_hi(i)
                act.wait_ge(s["ss_ready"], n_norm + 1)
                link(nc.scalar.activation(rstd[:, 0:n], bank(7, n), ACT.Ln, scale=1.0 / D, bias=eps))
                nc.scalar.activation(rstd[:, 0:n], rstd[:, 0:n], ACT.Exp, scale=-0.5).then_inc(s["rstd_ready"], 1)
                if shift:
                    for k in range(KC):
                        act.wait_ge(s["h_mul"], n_h + k + 1)
                        if splits:
                            nc.scalar.activation(hh_hi[:, k], h[:, k, 0:n], ACT.Identity, bias=shift(k))\
                                .then_inc(s["h_hi"], 1)
                        nc.scalar.activation(h[:, k, 0:n], h[:, k, 0:n], ACT.Identity, bias=shift(k))\
                            .then_inc(s["h_ready"], 1)

            def silu(u, par, n):
                w("up_done", u + 1, 16)
                nc.scalar.activation(sil[:, par, 0:n], bank(par, n), ACT.Silu).then_inc(s["silu_done"], 1)

            act.wait_ge(s["consts"], 32)
            nc.scalar.activation(cond[:], col("c", 0, KC), ACT.Silu).then_inc(s["cond_ready"], 1)
            act.wait_ge(s["table_ready"], 2)
            nc.scalar.activation(sin[:], sin[:], ACT.Sin).then_inc(s["rope_ready"], 1)
            nc.scalar.activation(cos[:], cos[:], ACT.Sin).then_inc(s["rope_ready"], 1)
            t = n_norm = n_h = 0
            for q, st in enumerate(stages):
                slab = slab_at[q]
                if st[0] == "ada":
                    continue
                n, scale, shift = norm_of(st)
                seq = split_seq(q, st)
                norm(q, n_norm, n_h, n, shift, seq[0:2])
                n_norm += 1
                n_h += KC
                if st[0] == "ffn":
                    for i in seq[2:5]:
                        split_hi(i)
                    for u in range(2 * t, 2 * (t + FFN_STEPS)):
                        if u % 2 == 0 and u > 2 * t:
                            a = u // 2 - t
                            for i in seq[2 + 3 * a:5 + 3 * a]:
                                split_hi(i)
                        if u >= 2:
                            act.wait_ge(s["hid_done"], u - 1)
                        silu(u, u % 2, n)
                    t += FFN_STEPS
                elif st[0] == "mix":
                    job = job_at[q]
                    qi, zs, nqk = view(QI, 12, T1 + 3), view(ZS, 4, T1), view(NQK, 7, T1)
                    for i, (kind, idx, _, _, eng) in enumerate(stage_jobs(st)[:30]):
                        if eng != "act":
                            continue
                        act.wait_ge(s["proj_done"], job + i + 1)
                        src = bank((job + i) % 4, T1)
                        if kind == "z":
                            ins = nc.scalar.activation(zs[:, idx], src, ACT.Silu)
                        else:
                            dst = {"qkv": lambda: qi[:, idx, 3:], "nq": lambda: nqk[:, idx],
                                   "nk": lambda: nqk[:, 4 + idx], "vc": lambda: view(VC, T1)}[kind]()
                            ins = nc.scalar.copy(dst, src)
                        ins.then_inc(s["proj_act"], 1)
                    gdn(q, st[1])
                    nsa_blocks(q, st[1], job)
                    hc, cb = view(HC, 2, 2 * NCMP), view(CB, 2)
                    for c in range(2):
                        act.wait_ge(s["proj_done"], job + 31 + c)
                        b = (job + 30 + c) % 4
                        mark(nc.scalar.copy(cb[:, c:c + 1], ps[:, b, 64:65]), q, "cb", c)
                        await_("act", q, "cb", c)
                        nc.scalar.activation(hc[:, c], ps[:, b, 0:2 * NCMP], ACT.Silu, bias=cb[:, c:c + 1])\
                            .then_inc(s["proj_act"], 1)
                    await_("pe", q, "kcmp")
                    for e in range(2):
                        nc.scalar.copy(view(KCMP, NCMP)[64 * e:64 * e + 64], ps[0:64, 4, e * NCMP:(e + 1) * NCMP])
                    await_("pe", q, "vcmp")
                    mark(nc.scalar.copy(view(VCMP, 2 * 64)[0:NCMP], ps[0:NCMP, 5, 0:2 * 64]), q, "cmp")
                    attention(q, st)
                    nsa_root(q)
                    take_outputs(q, st)
                elif st[0] == "fox":
                    fox_act(q, job_at[q])
                    fox_forget(q)
                    attention(q, st)
                    take_outputs(q, st)
                elif st[0] == "hg":
                    hg_act(q, job_at[q], st)
                elif st[0] == "moe":
                    moe_act(q, st[1], t)
                    t += 2 * NE

        @block.vector
        def _(dve):
            chain = [0]
            trip = [None]

            def w(name, value, per_trip):
                dve.wait_ge(s[name], value if trip[0] is None else trip[0] * per_trip + value)

            def link(ins):
                chain[0] += 1
                ins.then_inc(s["dve_chain"], 1)
                dve.wait_ge(s["dve_chain"], chain[0])

            def tick(ins):
                chain[0] += 1
                ins.then_inc(s["dve_chain"], 1)
                return chain[0]

            mark, await_ = stepper("dve")

            def conv(q, l):
                qi, qo = view(QI, 12, T1 + 3), view(QO, 12, T1)
                mark(nc.vector.memset(qi[:, :, 0:3], 0.0), q, "pad")
                await_("dve", q, "pad")
                for g in range(3):
                    for tap in range(4):
                        for c in range(4 * g, 4 * g + 4):
                            tapw = col("conv", (4 * l + tap) * 12 + c)
                            src = qi[:, c, tap:tap + T1]
                            if tap == 0:
                                dve.wait_ge(s["proj_act"], act_before(q) + c + 1)
                                ins = nc.vector.tensor_scalar(qo[:, c], src, tapw, None, ALU.mult)
                            else:
                                await_("dve", q, "tap", tap - 1, c)
                                ins = nc.vector.scalar_tensor_tensor(out=qo[:, c], in0=src, scalar=tapw, in1=qo[:, c],
                                                                     op0=ALU.mult, op1=ALU.add)
                            if tap < 3:
                                mark(ins, q, "tap", tap, c)
                    mark(ins, q, "conv", g)
                    for j in range(4 * g, 4 * g + 4):
                        ada_sum(slab_at[q] + 2 * j + 1, ada_before(q) + j)

            def y_out(q, st, job, first, n):
                for c in range(KC):
                    dve.wait_ge(s["proj_done"], job + first + c + 1)
                    src, xd = bank((job + first + c) % 4, n), x[:, c, T2 - n:T2]
                    if st[0] == "mix":
                        ins = nc.vector.scalar_tensor_tensor(out=xd, in0=src, scalar=gate_col(st[1], 1, c), in1=xd,
                                                             op0=ALU.mult, op1=ALU.add)
                    else:
                        ins = nc.vector.tensor_tensor(xd, src, xd, ALU.add)
                    ins.then_inc(s["proj_dve"], 1)

            def gdn(q, l, job):
                qo = view(QO, 12, T1)
                ba, sg, u8, sp, na = (view(SMALL, 2, 32), view(SMALL + 128, 2, 28), view(SMALL + 184, 2, 4),
                                      view(SMALL + 192, 2, 4), view(SMALL + 204, 2, 4))
                name, value = job_read[proj_end(q) - 1]
                dve.wait_ge(s[name], value)
                dtb = col("dt", l * GH, GH).rearrange("p (a n) -> p a n", a=1).to_broadcast([P, 2, GH])
                mark(nc.vector.tensor_tensor(u8, ba[:, :, 28:32], dtb, ALU.add), q, "u8")
                await_("dve", q, "u8")
                mark(nc.vector.scalar_tensor_tensor(out=na, in0=u8, scalar=-1.0, in1=u8, op0=ALU.mult, op1=ALU.min), q, "na")
                await_("act", q, "sg")
                mark(nc.vector.tensor_scalar(sg, sg, 1.0, None, ALU.add), q, "sg1")
                await_("dve", q, "sg1")
                mark(nc.vector.reciprocal(sg, sg), q, "sg")
                await_("act", q, "na")
                mark(nc.vector.scalar_tensor_tensor(out=sp, in0=u8, scalar=0.0, in1=na, op0=ALU.max, op1=ALU.add), q, "sp")
                await_("dve", q, "sp")
                await_("act", q, "ea")
                eab = view(SMALL + 200, 4).rearrange("p (a n) -> p a n", a=1).to_broadcast([P, 2, GH])
                mark(nc.vector.scalar_tensor_tensor(out=view(SMALL + 96, 2, 4), in0=sp, scalar=-1.0, in1=eab,
                                                    op0=ALU.mult, op1=ALU.mult), q, "g")
                for b in range(4):
                    await_("act", q, "rn", b)
                    r, v = sq[:, 2 * b:2 * b + 2, 0:T1], qo[:, 2 * b:2 * b + 2]
                    if b < 2:
                        ins = nc.vector.scalar_tensor_tensor(out=v, in0=v, scalar=float(P) ** -0.5, in1=r,
                                                             op0=ALU.mult, op1=ALU.mult)
                    else:
                        ins = nc.vector.tensor_tensor(v, v, r, ALU.mult)
                    if b < 3:
                        mark(ins, q, "unitn", b)
                await_("act", q, "qkv", 2)
                mark(ins, q, "k_ready")
                gc, gl = view(SMALL + 216, 8), view(SMALL + 224, 8)
                await_("pe", q, "gc")
                mark(nc.vector.tensor_copy(gc, ps[:, 6, 0:8]), q, "gc")
                await_("dve", q, "gc")
                dect, dd = view(DECT, 8, P), view(LL, 8, P)
                for t in range(2):
                    await_("pe", q, "gr", t)
                    for i in range(GH):
                        p = GH * t + i
                        nc.vector.tensor_scalar(dect[:, p], ps[:, 4 + t, i * P:(i + 1) * P], gc[:, p:p + 1], 0.0,
                                                ALU.subtract, ALU.min)
                        nc.vector.tensor_scalar(dd[:, p], ps[:, 4 + t, i * P:(i + 1) * P], gc[:, p:p + 1], 0.0,
                                                ALU.subtract, ALU.max)
                    last = ps[:, 4 + t, :].rearrange("p (a n) -> p a n", a=4)[:, :, P - 1]
                    mark(nc.vector.tensor_tensor(gl[:, 4 * t:4 * t + 4], last, gc[:, 4 * t:4 * t + 4], ALU.subtract),
                         q, "gr_read", t)
                bb, be = view(SMALL + 248, 2, 4), view(SMALL + 256, 8)
                mark(nc.vector.tensor_copy(bb, sg[:, :, 24:28]), q, "beta")
                await_("dve", q, "beta")
                await_("act", q, "egc")
                mark(nc.vector.tensor_tensor(be, view(SMALL + 248, 8), view(SMALL + 232, 8), ALU.mult), q, "be")
                await_("act", q, "ed")
                await_("dve", q, "be")
                kbe, vb, kd = view(KBE, 8, P), view(VB, 8, P), view(KD, 8, P)
                four = lambda b: ps[:, b, :].rearrange("p (a n) -> p a n", a=4)
                along = lambda at, t: view(at, 8)[:, 4 * t:4 * t + 4].rearrange("p (a n) -> p a n", n=1)\
                    .to_broadcast([P, 4, P])
                for t in range(2):
                    s4 = slice(4 * t, 4 * t + 4)
                    await_("pe", q, "vtok", t)
                    mark(nc.vector.tensor_tensor(vb[:, s4], four(2 + t), along(SMALL + 248, t), ALU.mult), q, "vb", t)
                    await_("pe", q, "ktok", t)
                    nc.vector.tensor_tensor(kd[:, s4], four(t), along(SMALL + 240, t), ALU.mult)
                    mark(nc.vector.tensor_tensor(kbe[:, s4], four(t), along(SMALL + 256, t), ALU.mult), q, "kbe", t)
                up4 = upper.rearrange("p (a n) -> p a n", a=1).to_broadcast([P, 4, P])
                st4 = cst("strict").rearrange("p (a n) -> p a n", a=1).to_broadcast([P, 4, P])
                for t in range(2):
                    s4 = slice(4 * t, 4 * t + 4)
                    await_("act", q, "dd", t)
                    mark(nc.vector.tensor_tensor(dd[:, s4], dd[:, s4], st4, ALU.mult), q, "dd", t)
                    await_("pe", q, "kk", t)
                    await_("dve", q, "dd", t)
                    for i in range(GH):
                        p = GH * t + i
                        ins = nc.vector.scalar_tensor_tensor(out=dd[:, p], in0=ps[:, 6 + t, i * P:(i + 1) * P],
                                                             scalar=view(SMALL + 248, 8)[:, p:p + 1], in1=dd[:, p],
                                                             op0=ALU.mult, op1=ALU.mult)
                    mark(ins, q, "l", t)
                tri, uu, lo = view(TT, 8, P), view(UU, 8, P), view(LO, 8, P)
                id8 = ident.rearrange("p (a n) -> p a n", a=1).to_broadcast([P, 8, P])
                nc.vector.tensor_copy(tri, id8)
                mark(nc.vector.tensor_copy(uu, id8), q, "unit")
                for lev in range(LEVELS):
                    m4 = cst("lev", lev * P).rearrange("p (a n) -> p a n", a=1).to_broadcast([P, 4, P])
                    for t in range(2):
                        s4 = slice(4 * t, 4 * t + 4)
                        await_("dve", q, "l", t)
                        if lev:
                            await_("pe", q, "p", lev - 1, t)
                        mark(nc.vector.tensor_tensor(lo[:, s4], dd[:, s4], m4, ALU.mult), q, "lo", lev, t)
                    if lev == 0:
                        for t in range(2):
                            s4 = slice(4 * t, 4 * t + 4)
                            await_("act", q, "dect", t)
                            mark(nc.vector.tensor_tensor(dect[:, s4], dect[:, s4], up4, ALU.mult), q, "dect", t)
                        egr = view(QE, 8, P)
                        for t in range(2):
                            s4 = slice(4 * t, 4 * t + 4)
                            await_("act", q, "eg", t)
                            mark(nc.vector.tensor_tensor(egr[:, s4], egr[:, s4], qo[:, 0:4, t * P:(t + 1) * P], ALU.mult),
                                 q, "qe", t)
                    for t in range(2):
                        s4 = slice(4 * t, 4 * t + 4)
                        await_("pe", q, "up", lev, t)
                        if lev < LEVELS - 1:
                            await_("pe", q, "tp", lev, t)
                        if lev:
                            await_("dve", q, "u", lev - 1, t)
                            await_("dve", q, "t", lev - 1, t)
                        else:
                            await_("dve", q, "unit")
                        mark(nc.vector.tensor_tensor(uu[:, s4], uu[:, s4], four(2 + t), ALU.subtract), q, "u", lev, t)
                        if lev < LEVELS - 1:
                            mark(nc.vector.tensor_tensor(tri[:, s4], tri[:, s4], four(4 + t), ALU.subtract),
                                 q, "t", lev, t)
                att = view(ATT, 8, P)
                for t in range(2):
                    s4 = slice(4 * t, 4 * t + 4)
                    await_("pe", q, "qk", t)
                    await_("dve", q, "dect", t)
                    mark(nc.vector.tensor_tensor(att[:, s4], dect[:, s4], four(6 + t), ALU.mult), q, "att", t)
                ot = view(OT, 4, T1)
                await_("act", q, "on")
                mark(nc.vector.scalar_tensor_tensor(out=ot, in0=ot, scalar=col("gdn_g", l), in1=sq[:, 0:4, 0:T1],
                                                    op0=ALU.mult, op1=ALU.mult), q, "on")
                await_("dve", q, "on")
                mark(nc.vector.tensor_tensor(h[:, 0:4, 0:T1], ot, view(ZS, 4, T1), ALU.mult), q, "y_gdn")

            def nsa_rope(q, l):
                nqk, tmp = view(NQK, 7, T1), view(RTMP, 2, T1)
                for b in range(4):
                    m = 2 if b < 3 else 1
                    two = lambda t: t.rearrange("p (a n) -> p a n", a=1).to_broadcast([P, m, T1])
                    v = nqk[:, 2 * b:2 * b + m]
                    await_("pe", q, "rot", b)
                    if b:
                        await_("dve", q, "roped", b - 1)
                    mark(nc.vector.tensor_tensor(tmp[:, 0:m], ps[:, 4 + b, 0:m * T1].rearrange("p (a n) -> p a n", a=m),
                                                 two(sin[:]), ALU.mult), q, "rtmp", b)
                    mark(nc.vector.tensor_tensor(v, v, two(cos[:]), ALU.mult), q, "rcos", b)
                    await_("dve", q, "rcos", b)
                    mark(nc.vector.tensor_tensor(v, v, tmp[:, 0:m], ALU.add), q, "roped", b)

            def attention(q, st):
                units = attn_units(st)
                pb, stat = view(PB, 2, 2, T2), view(STAT, 2, 3, 2)
                scale = 0.125 if st[0] == "mix" else 1.0
                fox = st[0] == "fox"
                chunks = KC if fox else 4
                oacc = view(OACC, 3 if fox else 2, chunks * P)

                def softmax_max(n):
                    br, i, j = units[n]
                    tiles, keys = attn_operands(st, br, i, j)[3:]
                    qn = tiles[i][1]
                    await_("pe", q, "s", n)
                    if n >= 2:
                        await_("pe", q, "turn", n - 2)
                    if keys == NCMP:
                        mask = cst("cneg", i * NCMP, NCMP)[0:qn]
                    elif qn < P:
                        mask = cst("negrow", T2 - P, qn)[0:qn]
                    else:
                        mask = cst("negrow", T2 - keys, keys)[0:qn]
                    b = n % 2 * 2
                    if fox:
                        for e in range(2):
                            ins = nc.vector.scalar_tensor_tensor(
                                out=pb[0:qn, n % 2, e, 0:keys], in0=ps[0:qn, b + e, 0:keys],
                                scalar=view(CQ, 3, FOXH)[0:qn, i, 2 * j + e:2 * j + e + 1], in1=mask,
                                op0=ALU.add, op1=ALU.add)
                    else:
                        m2 = mask.rearrange("p (a n) -> p a n", a=1).to_broadcast([qn, 2, keys])
                        ins = nc.vector.tensor_tensor(pb[0:qn, n % 2, :, 0:keys], ps[0:qn, b:b + 2, 0:keys], m2, ALU.add)
                    mark(ins, q, "sm", n)
                    await_("dve", q, "sm", n)
                    mark(nc.vector.tensor_reduce(stat[0:qn, n % 2, 0], pb[0:qn, n % 2, :, 0:keys], X_AXIS, ALU.max),
                         q, "mx", n)
                    await_("dve", q, "mx", n)
                    if keys == NCMP:
                        mark(nc.vector.tensor_scalar(stat[0:qn, n % 2, 1], stat[0:qn, n % 2, 0], -1e29, None, ALU.is_gt),
                             q, "any", n)
                        await_("dve", q, "any", n)
                        mark(nc.vector.tensor_tensor(stat[0:qn, n % 2, 0], stat[0:qn, n % 2, 0], stat[0:qn, n % 2, 1],
                                                     ALU.mult), q, "mx0", n)
                        await_("dve", q, "mx0", n)
                    mark(nc.vector.tensor_scalar(stat[0:qn, n % 2, 1], stat[0:qn, n % 2, 0], -scale, None, ALU.mult),
                         q, "nm", n)

                def output(n):
                    br, i, j = units[n]
                    tiles, keys = attn_operands(st, br, i, j)[3:]
                    qn = tiles[i][1]
                    den = stat[0:qn, n % 2, 2]
                    rd = view(STAT + 16, 2, 2)[0:qn, n % 2]
                    await_("act", q, "exp", n)
                    mark(nc.vector.tensor_scalar(rd, den, 1e-30, None, ALU.max), q, "den", n)
                    await_("dve", q, "den", n)
                    mark(nc.vector.reciprocal(rd, rd), q, "rden", n)
                    await_("dve", q, "rden", n)
                    if not fox:
                        gates = view(SMALL + 128, 2, 28)[0:qn, i, 3 * j + br:3 * j + br + 13:12]
                        mark(nc.vector.tensor_tensor(rd, rd, gates, ALU.mult), q, "gden", n)
                        await_("dve", q, "gden", n)
                    await_("pe", q, "pv", n)
                    for e in range(2):
                        o = oacc[0:qn, i, j * P + 64 * e:j * P + 64 * e + 64]
                        src = ps[0:qn, 6 + n % 2, 64 * e:64 * e + 64]
                        if br == 0:
                            ins = nc.vector.tensor_scalar(o, src, rd[:, e:e + 1], None, ALU.mult)
                        else:
                            if e == 0:
                                await_("dve", q, "o", units.index((br - 1, i, j)))
                            ins = nc.vector.scalar_tensor_tensor(out=o, in0=src, scalar=rd[:, e:e + 1], in1=o,
                                                                 op0=ALU.mult, op1=ALU.add)
                    mark(ins, q, "o", n)

                softmax_max(0)
                for n in range(len(units)):
                    if n + 1 < len(units):
                        softmax_max(n + 1)
                    output(n)
                await_("dve", q, "o", len(units) - 1)
                for i in range(0 if fox else 2):
                    o = oacc[:, i].rearrange("p (a n) -> p a n", a=8)
                    t8, r8 = view(PB, 8, 64), view(STAT + 32, 8)
                    await_("act", q, "exp", len(units) - 1)
                    if i:
                        await_("dve", q, "o_ready", i - 1)
                    mark(nc.vector.tensor_tensor(t8, o, o, ALU.mult), q, "osq2", i)
                    await_("dve", q, "osq2", i)
                    mark(nc.vector.tensor_reduce(r8, t8, X_AXIS, ALU.add), q, "oss", i)
                    await_("act", q, "orms", i)
                    mark(nc.vector.tensor_tensor(o, o, r8.rearrange("p (a n) -> p a n", n=1).to_broadcast([P, 8, 64]),
                                                 ALU.mult), q, "o_ready", i)

            def fox_qk(q, job):
                for c in range(2 * KC):
                    dve.wait_ge(s["proj_done"], job + c + 1)
                    nc.vector.tensor_copy(fox_chunk(c), bank((job + c) % 4, T2)).then_inc(s["proj_dve"], 1)
                for c in range(2 * KC):
                    await_("act", q, "frn", c)
                    g = (col("qg") if c < KC else col("kg"))
                    mark(nc.vector.scalar_tensor_tensor(out=fox_chunk(c), in0=fox_chunk(c), scalar=g,
                                                        in1=sq[:, c % 8, :], op0=ALU.mult, op1=ALU.mult), q, "fn", c)
                await_("dve", q, "fn", KC - 1)
                mark(nc.vector.tensor_scalar(view(FQ, KC, T2), view(FQ, KC, T2), 0.125, None, ALU.mult), q, "fqs")

            def fox_forget(q):
                lf, a, b = view(LF, 3, FOXH), view(LF + 48, 3, FOXH), view(LF + 96, 3, FOXH)
                for t, (at, size) in enumerate(KT2):
                    await_("pe", q, "fl", t)
                    mark(nc.vector.tensor_tensor(a[0:size, t], ps[0:size, 4 + t, 0:FOXH], col("fox_bf_row", 0, FOXH)[0:size],
                                                 ALU.add), q, "fu", t)
                    await_("dve", q, "fu", t)
                    mark(nc.vector.scalar_tensor_tensor(out=b[0:size, t], in0=a[0:size, t], scalar=-1.0, in1=a[0:size, t],
                                                        op0=ALU.mult, op1=ALU.min), q, "fabs", t)
                for t, (at, size) in enumerate(KT2):
                    await_("act", q, "fl", t)
                    mark(nc.vector.scalar_tensor_tensor(out=lf[0:size, t], in0=a[0:size, t], scalar=0.0, in1=b[0:size, t],
                                                        op0=ALU.min, op1=ALU.subtract), q, "lf", t)
                for t, (at, size) in enumerate(KT2):
                    await_("pe", q, "cq", t)
                    mark(nc.vector.tensor_copy(view(CQ, 3, FOXH)[0:size, t], ps[0:size, 4 + t, 0:FOXH]), q, "cqc", t)

            def hg_dve(q, job):
                hq, hk, hb, hgt = view(HQ, KC, T2), view(HK, KC, T2), view(HB, KC, T2), view(HG, KC, T2)
                lbs = view(HLB, 4, KC)
                mark(nc.vector.tensor_tensor(lbs[:, 2], col("hg_lb", 0, KC), col("hg_lb", KC, KC), ALU.max), q, "lbm")
                await_("dve", q, "lbm")
                nc.vector.tensor_tensor(lbs[:, 0], col("hg_lb", 0, KC), lbs[:, 2], ALU.subtract)
                mark(nc.vector.tensor_tensor(lbs[:, 1], col("hg_lb", KC, KC), lbs[:, 2], ALU.subtract), q, "lb0")
                await_("act", q, "lb")
                mark(nc.vector.tensor_tensor(lbs[:, 2], lbs[:, 0], lbs[:, 1], ALU.add), q, "lbs")
                await_("dve", q, "lbs")
                mark(nc.vector.reciprocal(lbs[:, 2], lbs[:, 2]), q, "lbr")
                await_("dve", q, "lbr")
                mark(nc.vector.tensor_tensor(lbs[:, 3], lbs[:, 0], lbs[:, 2], ALU.mult), q, "lbp0")
                mark(nc.vector.tensor_tensor(lbs[:, 2], lbs[:, 1], lbs[:, 2], ALU.mult), q, "lbp1")
                await_("dve", q, "lbp1")
                for c in range(KC):
                    dve.wait_ge(s["proj_act"], act_before(q) + KC + c + 1)
                    mark(nc.vector.tensor_scalar(hb[:, c], hk[:, c], lbs[:, 3, c:c + 1], lbs[:, 2, c:c + 1],
                                                 ALU.mult, ALU.add), q, "hf", c)
                for c in range(KC):
                    await_("dve", q, "hf", c)
                    mark(nc.vector.tensor_scalar(hk[:, c], hb[:, c], -1.0, 1.0, ALU.mult, ALU.add), q, "hk", c)
                for t, (at, n) in enumerate(KT2):
                    for c in range(KC):
                        await_("act", q, "lf", c)
                        ins = nc.vector.tensor_tensor_scan(hb[:, c, at:at + n], ones[:, 0:n], hb[:, c, at:at + n], 0.0,
                                                           ALU.mult, ALU.add)
                    mark(ins, q, "cum", t)
                e8, sc, kd, tmp = view(HE, 8, P), view(HSC, 8, P), view(HKD, 8, P), view(HTMP, 8, P)
                qeb, stt = view(HQE, 8, P), view(HST, 8, P)

                def masked(t, n, lev):
                    await_("pe", q, "hs", t, lev)
                    m = (ident if lev < 0 else cst("levT", lev * P))[0:n, 0:n]
                    m = m.rearrange("p (a n) -> p a n", a=1).to_broadcast([n, 8, n])
                    b = 2 * (lev % 2)
                    src = ps[0:n, b:b + 2, :].rearrange("p b (a n) -> p (b a) n", a=4)[:, :, 0:n]
                    if lev < 0:
                        if t:
                            await_("pe", q, "ho", t - 1)
                        mark(nc.vector.tensor_tensor(sc[0:n, :, 0:n], src, m, ALU.mult), q, "hmask", t, lev)
                        return
                    mark(nc.vector.tensor_tensor(tmp[0:n, :, 0:n], src, m, ALU.mult), q, "hmask", t, lev)
                    await_("dve", q, "hmask", t, lev)
                    mark(nc.vector.tensor_tensor(sc[0:n, :, 0:n], sc[0:n, :, 0:n], tmp[0:n, :, 0:n], ALU.add),
                         q, *(("hsum", t) if lev == n.bit_length() - 2 else ("hacc", t, lev)))

                for t, (at, n) in enumerate(KT2):
                    levels = n.bit_length() - 1
                    await_("dve", q, "cum", t)
                    end = hb[:, :, at + n - 1:at + n].to_broadcast([P, 8, n])
                    if t:
                        await_("pe", q, "hkdt", t - 1)
                    mark(nc.vector.tensor_tensor(kd[:, :, 0:n], end, hb[:, :, at:at + n], ALU.subtract), q, "kdd", t)
                    await_("act", q, "hqe", t)
                    mark(nc.vector.tensor_tensor(qeb[:, :, 0:n], qeb[:, :, 0:n], hq[:, :, at:at + n], ALU.mult),
                         q, "hqe", t)
                    await_("act", q, "kdd", t)
                    mark(nc.vector.tensor_tensor(kd[:, :, 0:n], kd[:, :, 0:n], hk[:, :, at:at + n], ALU.mult),
                         q, "hkd", t)
                    for lev in range(levels):
                        sz = 1 << lev
                        split = lambda v: v.rearrange("p h (m a b) -> p h m a b", a=2, b=sz)
                        ev, bv = split(e8[:, :, 0:n]), split(hb[:, :, at:at + n])
                        if lev:
                            await_("pe", q, "hs", t, lev - 1)
                        elif t:
                            await_("pe", q, "hs", t - 1, KT2[t - 1][1].bit_length() - 2)
                        m = n // (2 * sz)
                        for half in range(2):
                            ref = bv[:, :, :, 0, sz - 1:sz].to_broadcast([P, 8, m, sz])
                            ins = nc.vector.tensor_tensor(ev[:, :, :, half], bv[:, :, :, half], ref, ALU.subtract)
                        mark(ins, q, "dif", t, lev)
                        masked(t, n, lev - 1)
                        await_("act", q, "ee", t, lev)
                        qv, kv = split(hq[:, :, at:at + n]), split(hk[:, :, at:at + n])
                        nc.vector.tensor_tensor(ev[:, :, :, 0], ev[:, :, :, 0], kv[:, :, :, 0], ALU.mult)
                        mark(nc.vector.tensor_tensor(ev[:, :, :, 1], ev[:, :, :, 1], qv[:, :, :, 1], ALU.mult),
                             q, "eq", t, lev)
                    masked(t, n, levels - 1)
                    if t < 2:
                        await_("pe", q, "hst", t)
                        for i in range(HGH):
                            src = ps[:, 4 + i // 4, i % 4 * P:(i % 4 + 1) * P]
                            if t == 0:
                                ins = nc.vector.tensor_copy(stt[:, i], src)
                            else:
                                await_("act", q, "heb")
                                ins = nc.vector.scalar_tensor_tensor(out=stt[:, i], in0=stt[:, i],
                                                                     scalar=view(HEB, 8)[:, i:i + 1], in1=src,
                                                                     op0=ALU.mult, op1=ALU.add)
                        mark(ins, q, "hst", t)
                ho = view(HO, KC, T2)
                await_("act", q, "hon")
                mark(nc.vector.scalar_tensor_tensor(out=ho, in0=ho, scalar=col("hg_og"), in1=sq[:], op0=ALU.mult,
                                                    op1=ALU.mult), q, "hon")
                await_("dve", q, "hon")
                mark(nc.vector.tensor_tensor(h[:], ho, hgt, ALU.mult), q, "y_hg")

            def sort_tokens(q, l):
                m3, oh = view(MM, 3, NE), view(OH, 3, 2, NE)
                starts, cnt = view(STARTS, NE), view(CNT, NE)
                slot_iota = cst("iota", 0, SLOTS)
                await_("pe", q, "count")
                mark(nc.vector.tensor_copy(cnt, ps[:, 7, 0:NE]), q, "cnt")
                await_("dve", q, "cnt")
                mark(nc.vector.tensor_tensor_scan(starts, ones[:, 0:NE], cnt, 0.0, ALU.mult, ALU.add), q, "ends")
                await_("dve", q, "ends")
                mark(nc.vector.tensor_tensor(starts, starts, cnt, ALU.subtract), q, "starts")
                mark(nc.vector.tensor_reduce(view(CNT + NE, 1), cnt, X_AXIS, ALU.max), q, "most")
                await_("dve", q, "most")
                ints = view(INTS, NE + 1).bitcast(I32)
                nc.vector.tensor_copy(ints[:, 0:NE], starts)
                mark(nc.vector.tensor_copy(ints[:, NE:NE + 1], view(CNT + NE, 1)), q, "ints")
                for t, (at, size) in enumerate(KT2):
                    r = view(RT + 160 * t, 160)[0:size]
                    pos, pr = view(POS, 3, NE)[0:size, t], view(PRD, 3, 2, NE)[0:size, t]
                    await_("pe", q, "rank", t)
                    mark(nc.vector.tensor_tensor(pos, ps[0:size, 4 + t, 0:NE], m3[0:size, t], ALU.subtract), q, "pos", t)
                    await_("dve", q, "pos", t)
                    mark(nc.vector.tensor_tensor(pos, pos, starts[0:size], ALU.add), q, "pos2", t)
                    await_("dve", q, "pos2", t)
                    both = pos.rearrange("p (a n) -> p a n", a=1).to_broadcast([size, 2, NE])
                    mark(nc.vector.tensor_tensor(pr, oh[0:size, t], both, ALU.mult), q, "prd", t)
                    await_("dve", q, "prd", t)
                    mark(nc.vector.tensor_reduce(r[:, 150:152], pr, X_AXIS, ALU.add), q, "slot", t)
                    await_("dve", q, "slot", t)
                    pm, pw = view(PM, 3, SLOTS)[0:size, t], view(PW, 3, SLOTS)[0:size, t]
                    tmp = view(PTMP, SLOTS)[0:size]
                    io = slot_iota[0:size]
                    if t:
                        await_("dve", q, "pw", t - 1)
                    mark(nc.vector.tensor_scalar(tmp, io, r[:, 151:152], r[:, 109:110], ALU.is_equal, ALU.mult), q, "pt", t)
                    mark(nc.vector.tensor_scalar(pw, io, r[:, 150:151], r[:, 108:109], ALU.is_equal, ALU.mult), q, "p1", t)
                    mark(nc.vector.tensor_scalar(pm, io, r[:, 150:151], None, ALU.is_equal), q, "p2", t)
                    await_("dve", q, "p2", t)
                    mark(nc.vector.tensor_tensor(pw, pw, tmp, ALU.add), q, "pw", t)
                    mark(nc.vector.scalar_tensor_tensor(out=pm, in0=io, scalar=r[:, 151:152], in1=pm, op0=ALU.is_equal,
                                                        op1=ALU.add), q, "pm", t)
                mark(nc.vector.memset(view(XS, KC, SLOTS + W)[:, :, SLOTS:], 0.0), q, "xpad")
                for c in range(5):
                    cn = min(P, SLOTS - c * P)
                    await_("pe", q, "gp", c)
                    mark(nc.vector.tensor_copy(view(GP, 5, T2)[0:cn, c], ps[0:cn, 4 + c % 3, 0:T2]), q, "gp", c)

            def sparse_dve(q, l, t0):
                mark2, await2 = stepper("dve", l)
                steps = 2 * NE

                def hidden_s(k):
                    t = t0 + k
                    w("silu_done", 2 * t + 2, 16)
                    if k >= 2:
                        w("y_done", KC * (t - 1), 8 * KC)
                    nc.vector.tensor_tensor(hid[:, k % 2, :, 0:W], ps[:, 2 + k % 2, 0:2 * W].rearrange("p (f n) -> p f n", f=2),
                                            sil[:, k % 2, 0:2 * W].rearrange("p (f n) -> p f n", f=2), ALU.mult)\
                        .then_inc(s["hid_done"], 2)

                def take(e):
                    at = dve.value_load(expert_at(e, trip[0]), min_val=0, max_val=SLOTS)
                    w("y_done", KC * (t0 + 2 * e + 2), 8 * KC)
                    if e:
                        w("y_added", KC * (t0 + 2 * e), 8 * KC)
                    ins = nc.vector.tensor_copy(view(YS, KC, SLOTS + W)[:, :, bass.ds(at, W)],
                                                ps[:, 4 + e % 2, :].rearrange("p (k n) -> p k n", k=KC))
                    if e < NE - 1:
                        ins.then_inc(s["y_added"], 2 * KC)
                    else:
                        mark2(ins, "ys")

                def step(k):
                    if k + 1 < steps:
                        hidden_s(k + 1)
                    if k % 2:
                        take(k // 2)

                hidden_s(0)
                for k in range(8):
                    step(k)
                with dve.Fori(0, steps // 8 - 2) as it:
                    trip[0] = it
                    for k in range(8, 16):
                        step(k)
                    trip[0] = None
                for k in range(steps - 8, steps):
                    step(k)
                for d in range(KC):
                    await2("pe", "y", d)
                    nc.vector.tensor_tensor(x[:, d], bank(d % 4, T2), x[:, d], ALU.add).then_inc(s["y_added"], 2)

            def route(q, l):
                for t, (at, size) in enumerate(KT2):
                    r = view(RT + 160 * t, 160)[0:size]
                    await_("pe", q, "logits", t)
                    mark(nc.vector.tensor_tensor(r[:, 0:36], ps[0:size, 4 + t, 0:36],
                                                 col("moe_b", 36 * l, 36)[0:size], ALU.add), q, "lg", t)
                    mark(nc.vector.memset(r[:, 40:44], NEG), q, "lpad", t)
                    await_("dve", q, "lpad", t)
                    mark(nc.vector.tensor_copy(r[:, 36:40], r[:, 0:4]), q, "lgrp", t)
                    await_("dve", q, "lgrp", t)
                    mark(nc.vector.max(r[:, 44:52], r[:, 36:44]), q, "gmax", t)
                    await_("dve", q, "gmax", t)
                    mark(nc.vector.max_index(r[:, 96:104].bitcast(U32), r[:, 44:52], r[:, 36:44]), q, "gidx", t)
                    mark(nc.vector.tensor_scalar(r[:, 60:61], r[:, 44:45], -1.0, None, ALU.mult), q, "gneg", t)
                    await_("dve", q, "gidx", t)
                    mark(nc.vector.tensor_copy(r[:, 104:105], r[:, 96:97].bitcast(U32)), q, "gf", t)
                    await_("dve", q, "gf", t)
                    mark(nc.vector.tensor_scalar(r[:, 52:56], cst("iota", 0, 4)[0:size], r[:, 104:105], None,
                                                 ALU.is_equal), q, "goh", t)
                    await_("dve", q, "goh", t)
                    oh = r[:, 52:56].rearrange("p (g e) -> p g e", e=1).to_broadcast([size, GROUPS, PER_GROUP])
                    mark(nc.vector.tensor_tensor(r[:, 112:144].rearrange("p (g e) -> p g e", g=GROUPS),
                                                 r[:, 4:36].rearrange("p (g e) -> p g e", g=GROUPS), oh, ALU.mult),
                         q, "esel", t)
                    await_("dve", q, "esel", t)
                    mark(nc.vector.tensor_reduce(r[:, 80:88], r[:, 112:144].rearrange("p (g e) -> p e g", g=GROUPS),
                                                 X_AXIS, ALU.add), q, "el", t)
                    await_("dve", q, "el", t)
                    mark(nc.vector.max(r[:, 88:96], r[:, 80:88]), q, "emax", t)
                    await_("dve", q, "emax", t)
                    mark(nc.vector.max_index(r[:, 96:104].bitcast(U32), r[:, 88:96], r[:, 80:88]), q, "eidx", t)
                    mark(nc.vector.tensor_scalar(r[:, 63:64], r[:, 88:89], -1.0, None, ALU.mult), q, "eneg", t)
                    await_("dve", q, "eidx", t)
                    mark(nc.vector.tensor_copy(r[:, 106:108], r[:, 96:98].bitcast(U32)), q, "ef", t)
                    await_("dve", q, "ef", t)
                    mark(nc.vector.scalar_tensor_tensor(out=r[:, 106:108], in0=r[:, 104:105].to_broadcast([size, 2]),
                                                        scalar=float(PER_GROUP), in1=r[:, 106:108], op0=ALU.mult,
                                                        op1=ALU.add), q, "top", t)
                for t, (at, size) in enumerate(KT2):
                    r = view(RT + 160 * t, 160)[0:size]
                    oh, io = view(OH, 3, 2, NE)[0:size, t], cst("iota", 0, NE)[0:size]
                    await_("dve", q, "top", t)
                    for j in range(2):
                        mark(nc.vector.tensor_scalar(oh[:, j], io, r[:, 106 + j:107 + j], None, ALU.is_equal),
                             q, "oh", t, j)
                    await_("dve", q, "oh", t, 1)
                    mark(nc.vector.tensor_tensor(view(MM, 3, NE)[0:size, t], oh[:, 0], oh[:, 1], ALU.add), q, "m", t)
                for t, (at, size) in enumerate(KT2):
                    r = view(RT + 160 * t, 160)[0:size]
                    await_("act", q, "pair", t)
                    mark(nc.vector.scalar_tensor_tensor(out=r[:, 108:109], in0=r[:, 62:63], scalar=1.0, in1=r[:, 61:62],
                                                        op0=ALU.add, op1=ALU.mult), q, "wd", t)
                    await_("dve", q, "wd", t)
                    mark(nc.vector.reciprocal(r[:, 108:109], r[:, 108:109]), q, "w1", t)
                    await_("dve", q, "w1", t)
                    mark(nc.vector.tensor_tensor(r[:, 109:110], r[:, 108:109], r[:, 62:63], ALU.mult), q, "w2", t)
                    await_("dve", q, "w2", t)
                    g, oh = view(GT, 3, NE)[0:size, t], view(OH, 3, 2, NE)[0:size, t]
                    mark(nc.vector.tensor_scalar(g, oh[:, 0], r[:, 108:109], None, ALU.mult), q, "g1", t)
                    await_("dve", q, "g1", t)
                    mark(nc.vector.scalar_tensor_tensor(out=g, in0=oh[:, 1], scalar=r[:, 109:110], in1=g, op0=ALU.mult,
                                                        op1=ALU.add), q, "gates", t)

            def dense_dve(q, l, t0):
                steps = 2 * NE

                def select_gates(e):
                    if e >= 2:
                        w(f"gb_ps{l}", e - 1, 4)
                    onehot = ident[0:NE, e:e + 1] if trip[0] is None else ident[0:NE, bass.ds(trip[0] * 4 + e, 1)]
                    nc.vector.tensor_scalar(view(GSEL, 2, T2)[0:NE, e % 2], view(GTT, T2)[0:NE], onehot, None,
                                            ALU.mult).then_inc(s[f"gb_in{l}"], 1)

                def gated(k):
                    t, par = t0 + k, k % 2
                    w(f"gb_ready{l}", k // 2 + 1, 4)
                    for f in range(2):
                        u = 2 * t + f
                        w("silu_done", u + 1, 16)
                        nc.vector.tensor_tensor(hid[:, par, f, 0:T2], bank(2 + f, T2), sil[:, f, 0:T2], ALU.mult)\
                            .then_inc(s[f"gated{l}"], 1)
                        w(f"gated{l}", 2 * k + f + 1, 16)
                        nc.vector.tensor_tensor(hid[:, par, f, 0:T2], hid[:, par, f, 0:T2],
                                                view(GBC, 2, T2)[:, k // 2 % 2], ALU.mult).then_inc(s["hid_done"], 1)

                def step(k):
                    if k + 1 < steps:
                        if (k + 1) % 2 == 0 and (k + 1) // 2 + 1 < NE:
                            select_gates((k + 1) // 2 + 1)
                        gated(k + 1)
                    y_add(t0 + k, T2, None, first=(t0 + k == 0))

                select_gates(0)
                select_gates(1)
                gated(0)
                for k in range(8):
                    step(k)
                with dve.Fori(0, steps // 8 - 2) as it:
                    trip[0] = it
                    for k in range(8, 16):
                        step(k)
                    trip[0] = None
                for k in range(steps - 8, steps):
                    step(k)

            def moe_dve(q, l, t0):
                route(q, l)
                sort_tokens(q, l)
                await_("act", q, "gtt")
                await_("dve", q, "ints")
                most = dve.value_load(most_at, min_val=0, max_val=T2)
                with dve.If(most > W):
                    dense_dve(q, l, t0)
                with dve.Else():
                    sparse_dve(q, l, t0)

            def norm(n_norm, n_h, n, scale, shift, out, last):
                if last is not None:
                    for name, value in last:
                        dve.wait_ge(s[name], value)
                dve.wait_ge(s["rstd_ready"], n_norm + 1)
                for k in range(KC):
                    ins = nc.vector.scalar_tensor_tensor(out=out[:, k], in0=x[:, k, T2 - n:T2], scalar=scale(k),
                                                         in1=rstd[:, 0:n], op0=ALU.mult, op1=ALU.mult)
                    ins.then_inc(s["h_mul"], 1)

            def ada_sum(i, n):
                sum_slab(dve, ada_steps, i, n)

            def ada_col(l, lo, hi, slabs):
                dve.wait_ge(s["ada_ps"], slabs)
                nc.vector.tensor_tensor(mod[:, l, 2 * lo:2 * hi], ps[:, 6, 300:300 + 2 * (hi - lo)],
                                        col("ada_b", l * NADA + 2 * lo, 2 * (hi - lo)), ALU.add)\
                    .then_inc(s["ada_col"], 1)

            def split_lo(i):
                dve.wait_ge(s["w_hi"], split_at[i] + 1)
                wt = slab_view(i)
                nc.vector.tensor_tensor(low_view(i), wt, hi_slab(i).bitcast(F32), ALU.subtract)\
                    .then_inc(s["w_lo"], 1)

            def hidden_split(t, n):
                for f in range(2):
                    u = 2 * t + f
                    v, v_hi = hid[:, t % 2, f, 0:n], hid_hi[:, t % 2, f]
                    dve.wait_ge(s["silu_done"], u + 1)
                    link(nc.vector.tensor_tensor(v, sil[:, f, 0:n], bank(2 + f, n), ALU.mult))
                    link(nc.vector.tensor_copy(v_hi, v))
                    nc.vector.tensor_tensor(hid_lo[:, t % 2, f], v, v_hi.bitcast(F32), ALU.subtract)\
                        .then_inc(s["hid_done"], 1)

            def fold(l, i, n):
                dve.wait_ge(s["ada_col"], n)
                a = (3 * i + 1) * KC
                ins = nc.vector.scalar_tensor_tensor(out=mod[:, l, a:a + KC], in0=mod[:, l, a:a + KC], scalar=1.0,
                                                     in1=col("norm_g", (3 * l + i) * KC, KC), op0=ALU.add, op1=ALU.mult)
                v = tick(ins)
                if i != 1:
                    v = tick(nc.vector.tensor_scalar(mod[:, l, a + KC:a + 2 * KC], mod[:, l, a + KC:a + 2 * KC], 0.5,
                                                     None, ALU.mult))
                dve.wait_ge(s["dve_chain"], v)

            def y_add(t, n, gate, first=False):
                for d in range(KC):
                    w("y_done", KC * t + d + 1, 8 * KC)
                    if not first:
                        w("y_added", KC * (t - 1) + d + 1, 8 * KC)
                    xd = x[:, d, T2 - n:T2]
                    if gate is None:
                        ins = nc.vector.tensor_tensor(xd, bank(4 + d % 2, n), xd, ALU.add)
                    else:
                        ins = nc.vector.scalar_tensor_tensor(out=xd, in0=bank(4 + d % 2, n), scalar=gate(d), in1=xd,
                                                             op0=ALU.mult, op1=ALU.add)
                    ins.then_inc(s["y_added"], 1)

            def rope_tables():
                pos = arena[:, 0:T1].bitcast(I32)
                ang, turns, whole, r = (arena[:, T1 * i:T1 * (i + 1)] for i in range(1, 5))
                two_pi = 2 * np.pi
                hi = float(np.float32(6.28125))
                mid = float(np.float32(two_pi - hi))
                lo = float(np.float32(two_pi - hi - mid))
                magic = 12582912.0
                link(nc.vector.tensor_copy(ang, pos))
                link(nc.vector.tensor_scalar(ang, ang, cst("invf", 0, 1), None, ALU.mult))
                for out, quarter in ((sin, 0.0), (cos, 0.25)):
                    link(nc.vector.tensor_scalar(turns, ang, 1.0 / two_pi, quarter, ALU.mult, ALU.add))
                    link(nc.vector.tensor_scalar(whole, turns, magic, None, ALU.add))
                    link(nc.vector.tensor_scalar(whole, whole, magic, None, ALU.subtract))
                    link(nc.vector.scalar_tensor_tensor(out=r, in0=whole, scalar=-hi, in1=ang, op0=ALU.mult, op1=ALU.add))
                    link(nc.vector.scalar_tensor_tensor(out=r, in0=whole, scalar=-mid, in1=r, op0=ALU.mult, op1=ALU.add))
                    link(nc.vector.scalar_tensor_tensor(out=r, in0=whole, scalar=-lo, in1=r, op0=ALU.mult, op1=ALU.add))
                    link(nc.vector.tensor_scalar(r, r, quarter * two_pi, 3.1415925, ALU.add, ALU.min))
                    nc.vector.tensor_scalar(out[:], r, -3.1415925, None, ALU.max).then_inc(s["table_ready"], 1)

            ada_steps = [0]
            dve.wait_ge(s["consts"], 32)
            dve.wait_ge(s["pos_in"], 16)
            rope_tables()
            dve.wait_ge(s["cond_ready"], 1)
            dve.wait_ge(s["x_in"], 32)
            t = n_norm = n_ada = n_h = n_ready = ada_slabs = n_ffn = 0
            for q, st in enumerate(stages):
                if st[0] == "ada":
                    for a in range(st[2], st[3]):
                        if not by_pool(st, ada_slabs):
                            ada_sum(slab_at[q] + a - st[2], ada_slabs)
                        ada_slabs += 1
                    ada_col(st[1], st[2], st[3], ada_slabs)
                    n_ada += 1
                    continue
                n, scale, shift = norm_of(st)
                if st[0] in ("ffn", "mix"):
                    fold(st[1], 1 if st[0] == "mix" else 2 * st[2], n_ada)
                out = xs(n) if st[0] == "final" else h[:, :, 0:n]
                seq = split_seq(q, st)
                for i in seq[0:2]:
                    split_lo(i)
                norm(n_norm, n_h, n, scale, shift, out, [written[q]])
                n_norm += 1
                n_h += KC
                n_ready += KC if shift else 0
                if st[0] == "ffn":
                    gate = lambda d: gate_col(st[1], 2 * st[2], d)
                    for k in range(KC):
                        dve.wait_ge(s["h_ready"], n_ready - KC + k + 1)
                        dve.wait_ge(s["h_hi"], KC * n_ffn + k + 1)
                        nc.vector.tensor_tensor(hh_lo[:, k], h[:, k, 0:n], hh_hi[:, k].bitcast(F32), ALU.subtract)\
                            .then_inc(s["h_lo"], 1)
                    n_ffn += 1
                    for i in seq[2:5]:
                        split_lo(i)
                    hidden_split(t, n)
                    for a in range(FFN_STEPS):
                        for i in seq[5 + 3 * a:8 + 3 * a]:
                            split_lo(i)
                        if a + 1 < FFN_STEPS:
                            hidden_split(t + 1, n)
                        y_add(t, n, gate, first=(t == 0))
                        t += 1
                        layer, lo, hi = ada_share(st[1], st[2], a)
                        if a and hi > lo:
                            ada_col(layer, lo - 1, lo, ada_slabs)
                            n_ada += 1
                        ada_slabs += hi - lo
                    if hi > lo:
                        ada_col(layer, lo, hi, ada_slabs)
                        n_ada += 1
                elif st[0] == "moe":
                    moe_dve(q, st[1], t)
                    t += 2 * NE
                elif st[0] in ("mix", "fox", "hg"):
                    job = job_at[q]
                    if st[0] == "mix":
                        conv(q, st[1])
                        for i, (kind, idx, _, _, eng) in enumerate(stage_jobs(st)[:30]):
                            if eng == "dve":
                                dve.wait_ge(s["proj_done"], job + i + 1)
                                if kind == "vtok":
                                    ins = nc.vector.tensor_copy(view(VT, 2, 2, P)[:, idx[0], idx[1]],
                                                                bank((job + i) % 4, P))
                                else:
                                    ins = nc.vector.tensor_copy(view(SMALL, 2, 32)[:, idx], bank((job + i) % 4, 32))
                                ins.then_inc(s["proj_dve"], 1)
                        ada_slabs += ADA_PART
                        ada_col(st[1], 2 * ADA_PART, 3 * ADA_PART, ada_slabs)
                        n_ada += 1
                        nsa_rope(q, st[1])
                        gdn(q, st[1], job)
                        attention(q, st)
                    elif st[0] == "hg":
                        hg_dve(q, job)
                    else:
                        fox_qk(q, job)
                        fox_forget(q)
                        attention(q, st)
                    first = {"mix": 32, "fox": 28, "hg": 36}[st[0]]
                    y_out(q, st, job, first, n)


def kernel(**inputs):
    import concourse.bacc as bacc
    from concourse.bass_utils import run_bass_kernel_spmd

    stages = stage_list()
    arrays = host_arrays({k: np.asarray(v) for k, v in inputs.items()}, stages)
    noted = None
    for _ in range(2):
        nc = bacc.Bacc("TRN2", target_bir_lowering=False, num_devices=1)
        ap = {n: nc.dram_tensor(n, a.shape, mybir.dt.from_np(a.dtype), kind="ExternalInput").ap()
              for n, a in arrays.items()}
        ap["outT"] = nc.dram_tensor("outT", (P, KC * T1), F32, kind="ExternalOutput").ap()
        marks = Marks(noted)
        build(nc, ap, stages, marks)
        noted = marks.seen
    got = run_bass_kernel_spmd(nc, [arrays], core_ids=[0]).results[0]["outT"]
    return np.ascontiguousarray(got.reshape(P, KC, T1).transpose(2, 1, 0)).reshape(1, T1, D)
```
